# Optimizing a Trainium2 kernel written in Bass

```python
import jax, jax.numpy as jnp
from jax import lax
import numpy as np

D_MODEL = 1024
BATCH = 1
SEQ = 2048
DEPTH = 1

D_MIX = D_MODEL
D_POOL = D_MIX // 2
D_SGU = D_MIX - D_POOL
POOL_WINDOWS = (2, 4, 8, 16)
N_POOL_GROUPS = len(POOL_WINDOWS)
POOL_GROUP = D_POOL // N_POOL_GROUPS
N_SGU_HEADS = 4
SGU_HEAD = D_SGU // N_SGU_HEADS
CHUNK = 128
SPLITS = (D_POOL, 2 * D_POOL, 2 * D_POOL + D_SGU, 2 * D_POOL + 2 * D_SGU)
D_IN_PROJ = 2 * D_POOL + 3 * D_SGU
DEEPNORM_ALPHA = (2.0 * DEPTH) ** 0.25
DEEPNORM_BETA = (8.0 * DEPTH) ** -0.25
LN_EPS = 1e-5

kernel_name = "hybrid_pool_sgu_deepnorm_adaln"

def _layer_norm(x):
    xf = x.astype(jnp.float32)
    mu = jnp.mean(xf, axis=-1, keepdims=True)
    var = jnp.mean(jnp.square(xf - mu), axis=-1, keepdims=True)
    return ((xf - mu) * lax.rsqrt(var + LN_EPS)).astype(x.dtype)

def _pool_mixer(xa, w_pool, pool_scale):
    B, S, _ = xa.shape
    xg = xa.reshape(B, S, N_POOL_GROUPS, POOL_GROUP)
    cs = jnp.cumsum(xg.astype(jnp.float32), axis=1)
    cs = jnp.pad(cs, ((0, 0), (1, 0), (0, 0), (0, 0)))
    t = jnp.arange(S)
    pooled = []
    for g, w in enumerate(POOL_WINDOWS):
        lo = jnp.maximum(t + 1 - w, 0)
        cs_g = cs[:, :, g, :]
        win_sum = cs_g[:, 1:] - cs_g[:, lo]
        count = (t + 1 - lo).astype(jnp.float32)
        pooled.append(win_sum / count[None, :, None])
    pooled = jnp.stack(pooled, axis=2).astype(xa.dtype) - xg
    y = jnp.einsum('bsgc,gcd->bsgd', pooled, w_pool)
    return y.reshape(B, S, D_POOL) * pool_scale

def _sgu_mixer(u, v, ln_g, ln_b, w_s, b_s):
    B, S, _ = u.shape
    n_chunks = S // CHUNK
    v = v.reshape(B, n_chunks, CHUNK, N_SGU_HEADS, SGU_HEAD)
    v = _layer_norm(v) * ln_g + ln_b
    causal = jnp.tril(jnp.ones((CHUNK, CHUNK), dtype=bool))
    w = jnp.where(causal[None], w_s, 0)
    mixed = jnp.einsum('hts,bnshd->bnthd', w, v) + jnp.transpose(b_s)[:, :, None]
    return u * mixed.reshape(B, S, D_SGU)

def _hybrid_layer(x, c, w_ada, b_ada, w_in, w_pool, pool_scale,
                  sgu_ln_g, sgu_ln_b, w_sgu, b_sgu, w_out, ln_g, ln_b):
    mod = jax.nn.silu(c) @ w_ada + b_ada
    shift, scale, gate = jnp.split(mod, 3, axis=-1)
    h = _layer_norm(x) * (1 + scale[:, None]) + shift[:, None]
    proj = h @ w_in
    xa, ga, u, v, gb = jnp.split(proj, SPLITS, axis=-1)
    ya = _pool_mixer(xa, w_pool, pool_scale) * jax.nn.silu(ga)
    yb = _sgu_mixer(jax.nn.gelu(u, approximate=False), jax.nn.gelu(v, approximate=False),
                    sgu_ln_g, sgu_ln_b, w_sgu, b_sgu) * jax.nn.silu(gb)
    y = jnp.concatenate([ya, yb], axis=-1) @ w_out
    z = DEEPNORM_ALPHA * x + gate[:, None] * y
    return _layer_norm(z) * ln_g + ln_b

def setup_inputs(seed: int = 0) -> dict:
    key = jax.random.key(seed)
    ks = jax.random.split(key, 16)
    f32 = jnp.float32
    x = jax.random.normal(ks[0], (BATCH, SEQ, D_MODEL), f32)
    c = jax.random.normal(ks[1], (BATCH, D_MODEL), f32)
    w_ada = jax.random.normal(ks[2], (DEPTH, D_MODEL, 3 * D_MODEL), f32) * (0.5 * D_MODEL ** -0.5)
    b_ada = jax.random.normal(ks[3], (DEPTH, 3 * D_MODEL), f32) * 0.02
    w_in = jax.random.normal(ks[4], (DEPTH, D_MODEL, D_IN_PROJ), f32) * D_MODEL ** -0.5
    w_pool = jax.random.normal(ks[5], (DEPTH, N_POOL_GROUPS, POOL_GROUP, POOL_GROUP), f32) * POOL_GROUP ** -0.5
    pool_scale = 1.0 + 0.1 * jax.random.normal(ks[6], (DEPTH, D_POOL), f32)
    sgu_ln_g = 1.0 + 0.1 * jax.random.normal(ks[7], (DEPTH, N_SGU_HEADS, SGU_HEAD), f32)
    sgu_ln_b = 0.02 * jax.random.normal(ks[8], (DEPTH, N_SGU_HEADS, SGU_HEAD), f32)
    w_sgu = jax.random.normal(ks[9], (DEPTH, N_SGU_HEADS, CHUNK, CHUNK), f32) * CHUNK ** -0.5
    b_sgu = 1.0 + 0.1 * jax.random.normal(ks[10], (DEPTH, N_SGU_HEADS, CHUNK), f32)
    w_out = jax.random.normal(ks[11], (DEPTH, D_MIX, D_MODEL), f32) * (D_MIX ** -0.5 * DEEPNORM_BETA)
    ln_g = 1.0 + 0.1 * jax.random.normal(ks[12], (DEPTH, D_MODEL), f32)
    ln_b = 0.02 * jax.random.normal(ks[13], (DEPTH, D_MODEL), f32)
    return {"x": x, "c": c, "w_ada": w_ada, "b_ada": b_ada, "w_in": w_in,
            "w_pool": w_pool, "pool_scale": pool_scale, "sgu_ln_g": sgu_ln_g,
            "sgu_ln_b": sgu_ln_b, "w_sgu": w_sgu, "b_sgu": b_sgu, "w_out": w_out,
            "ln_g": ln_g, "ln_b": ln_b}

def reference(x, c, w_ada, b_ada, w_in, w_pool, pool_scale, sgu_ln_g, sgu_ln_b,
              w_sgu, b_sgu, w_out, ln_g, ln_b):
    for l in range(DEPTH):
        x = _hybrid_layer(x, c, w_ada[l], b_ada[l], w_in[l], w_pool[l], pool_scale[l],
                          sgu_ln_g[l], sgu_ln_b[l], w_sgu[l], b_sgu[l], w_out[l],
                          ln_g[l], ln_b[l])
    return x


_drawn_inputs = setup_inputs


def setup_inputs(seed=0):
    import zlib

    import numpy as np

    out = dict(_drawn_inputs(seed))
    spreads = {}
    factors = {'b_ada': 8.0,
     'pool_scale': 8.0,
     'sgu_ln_g': 8.0,
     'sgu_ln_b': 64.0,
     'b_sgu': 8.0,
     'ln_b': 2.772}
    for name, (base, spread) in spreads.items():
        noise = np.random.default_rng([zlib.crc32(name.encode()), seed]).standard_normal(out[name].shape)
        drawn = base * np.exp(spread * noise) if base else spread * noise
        out[name] = __import__('jax').numpy.asarray(drawn.astype(out[name].dtype))
    for name, factor in factors.items():
        out[name] = (out[name] * factor).astype(out[name].dtype)
    return out
```

```python
from contextlib import ExitStack

import concourse.bass as bass
from concourse import mybir

ALU = mybir.AluOpType
ACT = mybir.ActivationFunctionType
F32 = mybir.dt.float32
F32R = mybir.dt.float32r

P = 128
T = 512
TILES = T // P
G = 4
WINDOWS = (2, 4, 8, 16)
HALO = 16
EPS = 1e-5

V_UNITS = 4
IN_UNITS = V_UNITS + 4 * G
OUT_UNITS = 8
UNITS = IN_UNITS + OUT_UNITS
F_SLOTS = 2
S_SLOTS = 4
AHEAD = 2
MOD_COLS = 16
MOD_UNITS = 24
M_SLOTS = 4
V_C, V_SHIFT, V_SCALE, V_PS, V_LG, V_ROWS = 0, 8, 16, 24, 28, 32


class Steps:

    def __init__(self, sem, per_chunk):
        self.sem, self.per_chunk, self.n = sem, per_chunk, per_chunk

    def begin(self, chunk):
        assert self.n == self.per_chunk
        self.chunk, self.n = chunk, 0

    def then(self, eng, instruction):
        self.n += 1
        instruction.then_inc(self.sem, 1)
        eng.wait_ge(self.sem, self.chunk * self.per_chunk + self.n)


def hybrid_layer(nc, x, w_units, mod_units, vectors, b_gate, ln_g, ln_b, sgu_b, b_sgu, w_pool, w_sgu, out):
    D = x.shape[1]
    KT = D // P
    HALF = D // 2
    CHUNKS = x.shape[0] // T
    ALPHA = 2.0 ** 0.25
    assert D == 1024 and KT == 8 and CHUNKS >= 3 and UNITS % S_SLOTS == 0

    x_tiles = x.rearrange("(c j p) d -> c j p d", j=TILES, p=P)
    out_tiles = out.rearrange("(c j p) d -> c j p d", j=TILES, p=P)

    with ExitStack() as ctx:
        def sb(name, shape, dt=F32):
            return ctx.enter_context(nc.sbuf_tensor(name, shape, dt))

        def sem(name):
            return ctx.enter_context(nc.semaphore(name))

        hH, hL = sb("h_high", [P, KT, T], F32R), sb("h_low", [P, KT, T], F32R)
        yH, yL = sb("y_high", [P, KT, T], F32R), sb("y_low", [P, KT, T], F32R)
        wF = sb("w_float", [P, F_SLOTS, 1024])
        wH, wL = sb("w_high", [P, S_SLOTS, 1024], F32R), sb("w_low", [P, S_SLOTS, 1024], F32R)
        xn = sb("x_norm", [P, TILES, D])
        z = sb("z", [P, TILES, D])
        lngB, lnbB, gateB = sb("ln_g_rows", [P, D]), sb("ln_b_rows", [P, D]), sb("gate_rows", [P, D])
        gv = sb("v_gelu", [P, TILES, T])
        vH, vL = sb("v_high", [P, TILES, T], F32R), sb("v_low", [P, TILES, T], F32R)
        wtH, wtL = sb("w_sgu_high", [P, G, P], F32R), sb("w_sgu_low", [P, G, P], F32R)
        wpH, wpL = sb("w_pool_high", [P, G, P], F32R), sb("w_pool_low", [P, G, P], F32R)
        E = sb("sgu_bias", [P, G, P])
        ident, ones = sb("identity", [P, P]), sb("ones", [P, P])
        X = sb("xa", [P, HALO + T])
        S = [sb("sum_a", [P, HALO + T]), sb("sum_b", [P, HALO + T])]
        hF = [s[:, HALO:] for s in S]
        halo = sb("xa_halo", [P, G, HALO])
        pH, pL = sb("pooled_high", [P, T], F32R), sb("pooled_low", [P, T], F32R)
        tanh = sb("tanh", [P, T])
        sga, sgb = sb("gate_a", [P, T]), sb("gate_b", [P, T])
        ug = sb("u_gelu", [P, T])
        mixed = sb("mixed", [P, T])
        yP = sb("y_pool", [P, T])
        vec_rows = sb("vector_rows", [V_ROWS, P])
        cols = sb("vector_cols", [P, V_ROWS])
        ctanh = sb("c_tanh", [P, KT])
        csilu = sb("c_silu", [P, KT])
        modc = sb("mod_cols", [P, KT // 2, 4])
        halfc = sb("half_cols", [P, 2 * G])
        count_inv = sb("count_inv", [P, HALO])
        minus_half = sb("minus_half", [P, G])
        xst, xmv = sb("x_stats", [P, TILES, 2, 6]), sb("x_mean_var", [P, TILES, 2])
        zst, zmv = sb("z_stats", [P, TILES, 2, 6]), sb("z_mean_var", [P, TILES, 2])
        vst, vmv = sb("v_stats", [P, TILES, G, 6]), sb("v_mean_var", [P, TILES, G, 2])
        xve, xrs = sb("x_var_eps", [P, TILES]), sb("x_rstd", [P, TILES])
        zve, zrs = sb("z_var_eps", [P, TILES]), sb("z_rstd", [P, TILES])
        vve, vrs = sb("v_var_eps", [P, TILES, G]), sb("v_rstd", [P, TILES, G])
        spare = sb("spare", [P, 1])
        macc = gv
        wtF, wpF, sgubB, wsN = sga, sgb, mixed, yP
        bsgu_row, bgate_row = ug[0:1, :], z[0:1, 0, :]

        A = ctx.enter_context(nc.psum_tensor("bank_a", [P, 4, T], F32))
        B = ctx.enter_context(nc.psum_tensor("bank_b", [P, 4, T], F32))

        w_landed = [sem(f"w_landed{i}") for i in range(F_SLOTS)]
        m_landed = [sem(f"m_landed{i}") for i in range(M_SLOTS)]
        xn_landed = [sem(f"xn_landed{j}") for j in range(TILES)]
        z_landed = [sem(f"z_landed{j}") for j in range(TILES)]
        z_stored = [sem(f"z_stored{j}") for j in range(TILES)]
        vec_landed, small_landed, rows_landed = sem("vec_landed"), sem("small_landed"), sem("rows_landed")
        wsgu_landed, bgate_landed = sem("wsgu_landed"), sem("b_gate_landed")
        const_ready, ident_zero, mask_ready = sem("const_ready"), sem("ident_zero"), sem("mask_ready")
        x_rstd, v_rstd, z_rstd = sem("x_rstd_ready"), sem("v_rstd_ready"), sem("z_rstd_ready")
        w_high, w_low = sem("w_high_ready"), sem("w_low_ready")
        unit_done = sem("unit_done")
        vec_turned, vec_ready, c_tanh, c_ready = sem("vec_turned"), sem("vec_ready"), sem("c_tanh_ready"), sem("c_ready")
        mod_used, mod_summed, mod_ready = sem("mod_unit_used"), sem("mod_summed"), sem("mod_ready")
        wt_turned, wt_ready, e_done = sem("wt_turned"), sem("wt_ready"), sem("e_done")
        small_high, small_low = sem("small_high"), sem("small_low")
        gate_summed, gate_ready = sem("gate_summed"), sem("gate_ready")
        setup = Steps(sem("setup_steps"), 0)
        x_stats, x_ready, x_turned = sem("x_stats_ready"), sem("x_norm_ready"), sem("x_turned")
        h_float, h_high, h_low = sem("h_float_ready"), sem("h_high_ready"), sem("h_low_ready")
        v_gelu, v_stats, v_norm = sem("v_gelu_ready"), sem("v_stats_ready"), sem("v_norm_ready")
        v_high, v_low = sem("v_high_ready"), sem("v_low_ready")
        xa_copied, pooled, p_high, p_low = sem("xa_copied"), sem("pooled_ready"), sem("p_high_ready"), sem("p_low_ready")
        ga_tanh, ga_gated, gb_tanh, gb_gated = sem("ga_tanh"), sem("ga_gated"), sem("gb_tanh"), sem("gb_gated")
        u_gelu = sem("u_gelu_ready")
        pool_done, sgu_done = sem("pool_product_done"), sem("sgu_product_done")
        yp_ready, yp_high, yp_low = sem("yp_ready"), sem("yp_high_ready"), sem("yp_low_ready")
        ys_mixed, ys_ready, ys_high, ys_low = sem("sgu_mixed"), sem("ys_ready"), sem("ys_high_ready"), sem("ys_low_ready")
        z_added, z_stats, z_ready = sem("z_added"), sem("z_stats_ready"), sem("z_ready")
        pool_steps = Steps(sem("pool_steps"), sum(range(2, 2 + G)) + G)
        v_steps, x_steps = Steps(sem("v_steps"), 2 * TILES), Steps(sem("x_steps"), 2 * TILES)
        z_steps = [Steps(sem("z_first_half_steps"), TILES), Steps(sem("z_second_half_steps"), 4 * TILES)]

        def wait(eng, s, value):
            if not isinstance(value, int) or value > 0:
                eng.wait_ge(s, value)

        def run_chunks(eng, chunk):
            chunk(0, True, False)
            with eng.Fori(1, CHUNKS - 1) as c:
                chunk(c, False, False)
            chunk(CHUNKS - 1, False, True)

        block = ctx.enter_context(nc.Block())

        @block.sync
        def _(sp):
            def load_w(c, n):
                wait(sp, w_low, c * UNITS + n - F_SLOTS + 1)
                sp.dma_start(wF[:, n % F_SLOTS, :], w_units[n % UNITS]).then_inc(w_landed[n % F_SLOTS], 16)

            def load_m(m):
                wait(sp, mod_used, m - M_SLOTS + 1)
                sp.dma_start(z[:, m % M_SLOTS, :], mod_units[m]).then_inc(m_landed[m % M_SLOTS], 16)

            sp.dma_start(vec_rows[:, :], vectors).then_inc(vec_landed, 16)
            for j in range(TILES):
                sp.dma_start(xn[:, j, :], x_tiles[0, j]).then_inc(xn_landed[j], 16)
            for q in range(V_UNITS):
                for m in range(4 * q, 4 * q + 4):
                    load_m(m)
                load_w(0, q)
                if q == 1:
                    sp.dma_start(wsN[:, :].rearrange("p (h s) -> p h s", h=G),
                                 w_sgu.rearrange("h t s -> t h s")).then_inc(wsgu_landed, 16)
                    sp.dma_start(wpF[:, :].rearrange("p (g d) -> p g d", g=G),
                                 w_pool.rearrange("g c d -> c g d")).then_inc(small_landed, 16)
                    sp.dma_start(sgubB[:, :], sgu_b.broadcast_to([P, G * P])).then_inc(small_landed, 16)
                    sp.dma_start(bsgu_row, b_sgu).then_inc(small_landed, 16)

            def chunk(c, first, last):
                for n in range(UNITS):
                    if n + 2 * AHEAD < UNITS or not last:
                        load_w(c, n + 2 * AHEAD)
                    if first and n == 4:
                        sp.dma_start(lngB[:, :], ln_g.broadcast_to([P, D])).then_inc(rows_landed, 16)
                        sp.dma_start(lnbB[:, :], ln_b.broadcast_to([P, D])).then_inc(rows_landed, 16)
                    if first and 5 <= n < 5 + MOD_UNITS - MOD_COLS:
                        load_m(MOD_COLS + n - 5)
                    if first and n == 5 + MOD_UNITS - MOD_COLS:
                        sp.wait_ge(mod_used, MOD_UNITS - M_SLOTS + 1)
                        sp.dma_start(bgate_row, b_gate).then_inc(bgate_landed, 16)
                    if not first and 2 <= n < 2 + TILES:
                        j = n - 2
                        sp.wait_ge(z_ready, (c - 1) * TILES + j + 1)
                        sp.dma_start(out_tiles[c - 1, j], z[:, j, :]).then_inc(z_stored[j], 16)
                    if not last and 6 <= n < 6 + TILES:
                        j = n - 6
                        sp.wait_ge(x_turned, (c + 1) * KT)
                        sp.dma_start(xn[:, j, :], x_tiles[c + 1, j]).then_inc(xn_landed[j], 16)
                    if 17 <= n < 17 + TILES:
                        j = n - 17
                        if first:
                            sp.wait_ge(mod_used, MOD_UNITS)
                            sp.wait_ge(gate_summed, 2)
                        else:
                            sp.wait_ge(z_stored[j], c * 16)
                        sp.dma_start(z[:, j, :], x_tiles[c, j]).then_inc(z_landed[j], 16)

            run_chunks(sp, chunk)
            for j in range(TILES):
                sp.wait_ge(z_ready, (CHUNKS - 1) * TILES + j + 1)
                sp.dma_start(out_tiles[CHUNKS - 1, j], z[:, j, :]).then_inc(z_stored[j], 16)
            for j in range(TILES):
                sp.wait_ge(z_stored[j], CHUNKS * 16)

        @block.gpsimd
        def _(pool):
            nc.gpsimd.memset(ident[:, :], 0.0).then_inc(ident_zero, 1)
            nc.gpsimd.memset(ones[:, :], 1.0).then_inc(const_ready, 1)
            nc.gpsimd.memset(minus_half[:, :], -0.5).then_inc(const_ready, 1)
            nc.gpsimd.memset(halo[:, :, :], 0.0).then_inc(const_ready, 1)
            pool.wait_ge(ident_zero, 1)
            nc.gpsimd.affine_select(out=ident[:, :], in_=ident[:, :], compare_op=ALU.not_equal, fill=1.0, base=0,
                                    pattern=[[-1, P]], channel_multiplier=1).then_inc(const_ready, 1)

            def rstd(ready, var_eps, rstd_out, exponent):
                nc.gpsimd.tensor_tensor(rstd_out, var_eps, exponent, ALU.pow).then_inc(ready, 1)

            def x_rstds(c, j):
                pool.wait_ge(x_stats, c * TILES + j + 1)
                rstd(x_rstd, xve[:, j:j + 1], xrs[:, j:j + 1], minus_half[:, 0:1])

            pool.wait_ge(const_ready, 4)
            for j in range(TILES):
                x_rstds(0, j)
            for t in range(HALO):
                nc.gpsimd.memset(count_inv[:, t:t + 1], 1.0 / (t + 1)).then_inc(const_ready, 1)
            pool.wait_ge(wsgu_landed, 16)
            ws = wsN[:, :].rearrange("p (h s) -> p h s", h=G)
            nc.gpsimd.affine_select(out=ws, in_=ws, compare_op=ALU.is_ge, fill=0.0, base=0,
                                    pattern=[[0, G], [-1, P]], channel_multiplier=1).then_inc(mask_ready, 1)

            def z_rstds(c, j):
                pool.wait_ge(z_stats, c * TILES + j + 1)
                rstd(z_rstd, zve[:, j:j + 1], zrs[:, j:j + 1], minus_half[:, 0:1])

            def chunk(c, first, last):
                if not first:
                    for j in range(TILES):
                        z_rstds(c - 1, j)
                for j in range(TILES):
                    pool.wait_ge(v_stats, c * TILES + j + 1)
                    rstd(v_rstd, vve[:, j, :], vrs[:, j, :], minus_half[:, :])
                if not last:
                    for j in range(TILES):
                        x_rstds(c + 1, j)

            run_chunks(pool, chunk)
            for j in range(TILES):
                z_rstds(CHUNKS - 1, j)

        @block.scalar
        def _(act):
            def split_high(c, n):
                wait(act, unit_done, c * UNITS + n - S_SLOTS + 1)
                act.wait_ge(w_landed[n % F_SLOTS], (c * (UNITS // F_SLOTS) + n // F_SLOTS + 1) * 16)
                nc.scalar.activation(wH[:, n % S_SLOTS, :], wF[:, n % F_SLOTS, :], ACT.Copy).then_inc(w_high, 1)

            def h_evacuate(c, k):
                act.wait_ge(x_turned, c * KT + k + 1)
                wait(act, h_low, c * KT + k - 1)
                bank = B[:, k % 3 if isinstance(c, int) and c == 0 else k % 4, :]
                shift, scale = modc[:, k // 2, k % 2:k % 2 + 1], modc[:, k // 2, 2 + k % 2:3 + k % 2]
                nc.scalar.activation(hF[k % 2], bank, ACT.Identity, bias=shift, scale=scale).then_inc(h_float, 1)
                nc.scalar.activation(hH[:, k, :], bank, ACT.Identity, bias=shift, scale=scale).then_inc(h_high, 1)

            act.wait_ge(vec_turned, 1)
            nc.scalar.activation(cols[:, :], B[:, 3, 0:V_ROWS], ACT.Copy).then_inc(vec_ready, 1)
            act.wait_ge(vec_ready, 1)
            nc.scalar.activation(ctanh[:, :], cols[:, V_C:V_C + KT], ACT.Tanh, scale=0.5).then_inc(c_tanh, 1)
            for q in range(V_UNITS):
                act.wait_ge(mod_ready, q + 1)
                h_evacuate(0, 2 * q)
                split_high(0, q)
                h_evacuate(0, 2 * q + 1)
            act.wait_ge(wt_turned, 1)
            nc.scalar.activation(wtF[:, :], B[:, 3, :], ACT.Copy).then_inc(wt_ready, 1)
            nc.scalar.activation(wtH[:, :, :].rearrange("p h t -> p (h t)"), B[:, 3, :], ACT.Copy).then_inc(small_high, 1)
            act.wait_ge(small_landed, 48)
            nc.scalar.activation(wpH[:, :, :].rearrange("p g d -> p (g d)"), wpF[:, :], ACT.Copy).then_inc(small_high, 1)
            act.wait_ge(e_done, 1)
            nc.scalar.activation(E[:, :, :].rearrange("p h t -> p (h t)"), B[:, 3, :], ACT.Copy, scale=0.5)\
                .then_inc(small_high, 1)

            def chunk(c, first, last):
                for n in range(UNITS):
                    if (n + AHEAD < UNITS or not last) and not (first and n + AHEAD < V_UNITS):
                        split_high(c, n + AHEAD)
                    if n == V_UNITS:
                        act.wait_ge(unit_done, c * UNITS + V_UNITS)
                        for j in range(TILES):
                            nc.scalar.activation(gv[:, j, :], A[:, j, :], ACT.Gelu).then_inc(v_gelu, 1)
                    g, step = (n - V_UNITS - 1) // 4, (n - V_UNITS - 1) % 4
                    if n > V_UNITS and g < G:
                        act.wait_ge(unit_done, c * UNITS + n)
                        if step == 0:
                            wait(act, pooled, c * G + g)
                            nc.scalar.activation(X[:, HALO:], B[:, 0, :], ACT.Copy).then_inc(xa_copied, 1)
                        if step == 1:
                            nc.scalar.activation(tanh[:, :], B[:, 1, :], ACT.Tanh, scale=0.5).then_inc(ga_tanh, 1)
                            act.wait_ge(pooled, c * G + g + 1)
                            nc.scalar.activation(pH[:, :], S[(g + 1) % 2][:, HALO:], ACT.Copy).then_inc(p_high, 1)
                        if step == 2:
                            wait(act, ys_mixed, c * G + g)
                            nc.scalar.activation(ug[:, :], B[:, 2, :], ACT.Gelu).then_inc(u_gelu, 1)
                        if step == 3:
                            act.wait_ge(ga_gated, c * G + g + 1)
                            nc.scalar.activation(tanh[:, :], B[:, 3, :], ACT.Tanh, scale=0.5).then_inc(gb_tanh, 1)
                            act.wait_ge(yp_ready, c * G + g + 1)
                            nc.scalar.activation(yH[:, g, :], yP[:, :], ACT.Copy).then_inc(yp_high, 1)
                            act.wait_ge(ys_ready, c * G + g + 1)
                            nc.scalar.activation(yH[:, G + g, :], mixed[:, :], ACT.Copy).then_inc(ys_high, 1)
                    if V_UNITS < n <= V_UNITS + 2:
                        for j in range(2 * (n - V_UNITS - 1), 2 * (n - V_UNITS)):
                            act.wait_ge(v_norm, c * TILES + j + 1)
                            nc.scalar.activation(vH[:, j, :], gv[:, j, :], ACT.Copy).then_inc(v_high, 1)
                    if first and n == IN_UNITS - 1:
                        act.wait_ge(gate_summed, 2)
                        for half in range(2):
                            nc.scalar.activation(gateB[:, half * HALF:(half + 1) * HALF], A[:, 2 * half, :], ACT.Copy)\
                                .then_inc(gate_ready, 1)
                    if not last and IN_UNITS <= n < IN_UNITS + 4:
                        for k in range(2 * (n - IN_UNITS), 2 * (n - IN_UNITS) + 2):
                            h_evacuate(c + 1, k)

            run_chunks(act, chunk)

        @block.vector
        def _(dve):
            vec = nc.vector

            def split_low(c, n):
                dve.wait_ge(w_high, c * UNITS + n + 1)
                vec.tensor_tensor(wL[:, n % S_SLOTS, :], wF[:, n % F_SLOTS, :],
                                  wH[:, n % S_SLOTS, :].bitcast(F32), ALU.subtract).then_inc(w_low, 1)

            def h_split(c, k):
                dve.wait_ge(h_high, c * KT + k + 1)
                vec.tensor_tensor(hL[:, k, :], hF[k % 2], hH[:, k, :].bitcast(F32), ALU.subtract).then_inc(h_low, 1)

            def aggregate(steps, out_stats, in_stats, last_stats):
                steps.then(dve, last_stats)
                vec.memset(spare[:, :], 0.0)
                for o, i in zip(out_stats, in_stats):
                    last = vec.bn_aggr(o, i)
                steps.then(dve, last)

            def x_stats_of(c, j):
                dve.wait_ge(xn_landed[j], (c + 1) * 16)
                for h in range(2):
                    last = vec.bn_stats(xst[:, j, h, :], xn[:, j, h * HALF:(h + 1) * HALF])
                aggregate(x_steps, [xmv[:, j, :]], [xst[:, j, :, :].rearrange("p a b -> p (a b)")], last)
                vec.tensor_scalar(xve[:, j:j + 1], xmv[:, j, 1:2], EPS, None, ALU.add).then_inc(x_stats, 1)

            def x_norm_of(c, j):
                dve.wait_ge(x_rstd, c * TILES + j + 1)
                vec.tensor_scalar(xn[:, j, :], xn[:, j, :], xmv[:, j, 0:1], xrs[:, j:j + 1],
                                  ALU.subtract, ALU.mult).then_inc(x_ready, 1)

            def mod_sum(m):
                dve.wait_ge(m_landed[m % M_SLOTS], (m // M_SLOTS + 1) * 16)
                unit = z[:, m % M_SLOTS, :]
                if m < MOD_COLS:
                    parts = [(macc[:, m // 4, :], unit[:, a * T:(a + 1) * T], 2 * (m % 4) + a) for a in range(2)]
                else:
                    parts = [(gateB[:, :], unit, m - MOD_COLS)]
                for n, (acc, rows, k) in enumerate(parts):
                    c_col = csilu[:, k:k + 1]
                    if k == 0:
                        ins = vec.tensor_scalar(acc, rows, c_col, None, ALU.mult)
                    else:
                        ins = vec.scalar_tensor_tensor(out=acc, in0=rows, scalar=c_col, in1=acc,
                                                       op0=ALU.mult, op1=ALU.add)
                    if n < len(parts) - 1:
                        setup.then(dve, ins)
                ins.then_inc(mod_used, 1)
                dve.wait_ge(mod_used, m + 1)

            setup.begin(0)
            x_steps.begin(0)
            for j in range(TILES):
                x_stats_of(0, j)
                if j == 0:
                    dve.wait_ge(vec_ready, 1)
                    dve.wait_ge(c_tanh, 1)
                    setup.then(dve, vec.scalar_tensor_tensor(out=csilu[:, :], in0=ctanh[:, :], scalar=1.0,
                                                             in1=cols[:, V_C:V_C + KT], op0=ALU.add, op1=ALU.mult))
                    vec.tensor_scalar(csilu[:, :], csilu[:, :], 0.5, None, ALU.mult).then_inc(c_ready, 1)
                    vec.tensor_scalar(halfc[:, :], cols[:, V_PS:V_PS + 2 * G], 0.5, None, ALU.mult).then_inc(c_ready, 1)
                    vec.tensor_scalar(cols[:, V_SCALE:V_SCALE + KT], cols[:, V_SCALE:V_SCALE + KT], 1.0, None,
                                      ALU.add).then_inc(c_ready, 1)
                else:
                    x_norm_of(0, j - 1)
            x_norm_of(0, TILES - 1)
            dve.wait_ge(c_ready, 3)
            for q in range(V_UNITS):
                for m in range(4 * q, 4 * q + 4):
                    mod_sum(m)
                dve.wait_ge(mod_summed, q + 1)
                bias = cols[:, V_SHIFT:V_SHIFT + 2 * KT].rearrange("p (s k) -> p s k", s=2)[:, :, 2 * q:2 * q + 2]
                vec.tensor_tensor(modc[:, q, :].rearrange("p (s k) -> p s k", s=2),
                                  B[:, 3, 0:4].rearrange("p (s k) -> p s k", s=2), bias, ALU.add).then_inc(mod_ready, 1)
                h_split(0, 2 * q)
                split_low(0, q)
                h_split(0, 2 * q + 1)
            dve.wait_ge(small_high, 2)
            vec.tensor_tensor(wtL[:, :, :].rearrange("p h t -> p (h t)"), wtF[:, :],
                              wtH[:, :, :].rearrange("p h t -> p (h t)").bitcast(F32), ALU.subtract).then_inc(small_low, 1)
            vec.tensor_tensor(wpL[:, :, :].rearrange("p g d -> p (g d)"), wpF[:, :],
                              wpH[:, :, :].rearrange("p g d -> p (g d)").bitcast(F32), ALU.subtract).then_inc(small_low, 1)

            def pooling(c, g, first):
                w = WINDOWS[g]
                if g == 0 and first:
                    dve.wait_ge(const_ready, 4 + HALO)
                wait(dve, p_low, c * G + g)
                wait(dve, h_low, (c + 1) * KT)
                dve.wait_ge(xa_copied, c * G + g + 1)
                pool_steps.then(dve, vec.tensor_copy(X[:, 0:HALO], halo[:, g, :]))
                src = X
                for level in range(g + 1):
                    shift = 1 << level
                    lo = HALO - (w - 2 * shift)
                    dst = S[level % 2]
                    pool_steps.then(dve, vec.tensor_tensor(dst[:, lo:], src[:, lo:],
                                                           src[:, lo - shift:HALO + T - shift], ALU.add))
                    src = dst
                dst = S[(g + 1) % 2]
                vec.tensor_copy(halo[:, g, :], X[:, T:])
                mean = vec.scalar_tensor_tensor(out=dst[:, HALO:], in0=src[:, HALO:], scalar=1.0 / w,
                                                in1=X[:, HALO:], op0=ALU.mult, op1=ALU.subtract)
                if first:
                    head = slice(HALO, HALO + w - 1)
                    setup.then(dve, mean)
                    setup.then(dve, vec.tensor_tensor(dst[:, head], src[:, head], count_inv[:, 0:w - 1], ALU.mult))
                    mean = vec.tensor_tensor(dst[:, head], dst[:, head], X[:, head], ALU.subtract)
                mean.then_inc(pooled, 1)

            def pooled_low(c, g):
                dve.wait_ge(p_high, c * G + g + 1)
                vec.tensor_tensor(pL[:, :], S[(g + 1) % 2][:, HALO:], pH[:, :].bitcast(F32), ALU.subtract).then_inc(p_low, 1)

            def gate(tanh_ready, gated, out_t, bank, value):
                dve.wait_ge(tanh_ready, value)
                vec.scalar_tensor_tensor(out=out_t[:, :], in0=tanh[:, :], scalar=1.0, in1=B[:, bank, :],
                                         op0=ALU.add, op1=ALU.mult).then_inc(gated, 1)

            def y_pool(c, g):
                dve.wait_ge(pool_done, c * G + g + 1)
                wait(dve, yp_high, c * G + g)
                dve.wait_ge(ga_gated, c * G + g + 1)
                vec.scalar_tensor_tensor(out=yP[:, :], in0=A[:, g % 2, :], scalar=halfc[:, g:g + 1], in1=sga[:, :],
                                         op0=ALU.mult, op1=ALU.mult).then_inc(yp_ready, 1)

            def mix(c, g, first):
                dve.wait_ge(sgu_done, c * G + g + 1)
                wait(dve, ys_high, c * G + g)
                if first and g == 0:
                    dve.wait_ge(small_high, 3)
                tiles = "p (j t) -> p j t"
                bias = E[:, g:g + 1, :].broadcast_to([P, TILES, P])
                pool_steps.then(dve, vec.scalar_tensor_tensor(
                    out=mixed[:, :].rearrange(tiles, j=TILES), in0=A[:, 2 + g % 2, :].rearrange(tiles, j=TILES),
                    scalar=halfc[:, G + g:G + g + 1], in1=bias, op0=ALU.mult, op1=ALU.add))
                dve.wait_ge(u_gelu, c * G + g + 1)
                vec.tensor_tensor(mixed[:, :], mixed[:, :], ug[:, :], ALU.mult).then_inc(ys_mixed, 1)

            def y_low(c, g, high, low, row, src):
                dve.wait_ge(high, c * G + g + 1)
                vec.tensor_tensor(yL[:, row, :], src[:, :], yH[:, row, :].bitcast(F32), ALU.subtract).then_inc(low, 1)

            def v_stats_of(c, j):
                dve.wait_ge(v_gelu, c * TILES + j + 1)
                for h in range(G):
                    last = vec.bn_stats(vst[:, j, h, :], gv[:, j, h * P:(h + 1) * P])
                aggregate(v_steps, [vmv[:, j, h, :] for h in range(G)], [vst[:, j, h, :] for h in range(G)], last)
                vec.tensor_scalar(vve[:, j, :], vmv[:, j, :, 1], EPS, None, ALU.add).then_inc(v_stats, 1)

            def v_norm_of(c, j):
                dve.wait_ge(v_rstd, c * TILES + j + 1)
                for h in range(G):
                    head = gv[:, j, h * P:(h + 1) * P]
                    last = vec.tensor_scalar(head, head, vmv[:, j, h, 0:1], vrs[:, j, h:h + 1], ALU.subtract, ALU.mult)
                last.then_inc(v_norm, 1)

            def v_low_of(c, j):
                dve.wait_ge(v_high, c * TILES + j + 1)
                vec.tensor_tensor(vL[:, j, :], gv[:, j, :], vH[:, j, :].bitcast(F32), ALU.subtract).then_inc(v_low, 1)

            def z_half(c, j, half, bank):
                cut = slice(half * HALF, (half + 1) * HALF)
                if half == 0:
                    dve.wait_ge(z_landed[j], (c + 1) * 16)
                product = vec.tensor_tensor(tanh[:, :], bank[:, j, :], gateB[:, cut], ALU.mult)
                product.then_inc(z_added, 1)
                dve.wait_ge(z_added, c * 2 * TILES + half * TILES + j + 1)
                z_steps[half].then(dve, vec.scalar_tensor_tensor(out=z[:, j, cut], in0=z[:, j, cut], scalar=ALPHA,
                                                                 in1=tanh[:, :], op0=ALU.mult, op1=ALU.add))
                stats = vec.bn_stats(zst[:, j, half, :], z[:, j, cut])
                if half:
                    aggregate(z_steps[1], [zmv[:, j, :]], [zst[:, j, :, :].rearrange("p a b -> p (a b)")], stats)
                    vec.tensor_scalar(zve[:, j:j + 1], zmv[:, j, 1:2], EPS, None, ALU.add).then_inc(z_stats, 1)

            def z_norm(c, j):
                dve.wait_ge(z_rstd, c * TILES + j + 1)
                z_steps[1].then(dve, vec.scalar_tensor_tensor(out=z[:, j, :], in0=z[:, j, :], scalar=zmv[:, j, 0:1],
                                                              in1=lngB[:, :], op0=ALU.subtract, op1=ALU.mult))
                vec.scalar_tensor_tensor(out=z[:, j, :], in0=z[:, j, :], scalar=zrs[:, j:j + 1], in1=lnbB[:, :],
                                         op0=ALU.mult, op1=ALU.add).then_inc(z_ready, 1)

            def chunk(c, first, last):
                for steps in (pool_steps, v_steps, z_steps[0]):
                    steps.begin(c)
                if not first:
                    z_steps[1].begin(c - 1)
                if not last:
                    x_steps.begin(c + 1)
                for n in range(UNITS):
                    if (n + AHEAD < UNITS or not last) and not (first and n + AHEAD < V_UNITS):
                        split_low(c, n + AHEAD)
                    if not first and n < TILES + 1:
                        if n < TILES:
                            if n == 0:
                                dve.wait_ge(unit_done, c * UNITS)
                            z_half(c - 1, n, 1, B)
                        if n > 0:
                            z_norm(c - 1, n - 1)
                    if n == V_UNITS:
                        v_stats_of(c, 0)
                        v_stats_of(c, 1)
                        v_norm_of(c, 0)
                    g, step = (n - V_UNITS - 1) // 4, (n - V_UNITS - 1) % 4
                    if n > V_UNITS and g < G:
                        if step == 0:
                            pooling(c, g, first)
                        if step == 1:
                            pooled_low(c, g)
                            gate(ga_tanh, ga_gated, sga, 1, c * G + g + 1)
                        if step == 2:
                            y_pool(c, g)
                            if g > 0:
                                mix(c, g, first)
                        if step == 3:
                            gate(gb_tanh, gb_gated, sgb, 3, c * G + g + 1)
                            if g == 0:
                                mix(c, g, first)
                            y_low(c, g, yp_high, yp_low, g, yP)
                            dve.wait_ge(ys_mixed, c * G + g + 1)
                            dve.wait_ge(gb_gated, c * G + g + 1)
                            vec.tensor_tensor(mixed[:, :], mixed[:, :], sgb[:, :], ALU.mult).then_inc(ys_ready, 1)
                            y_low(c, g, ys_high, ys_low, G + g, mixed)
                    if n == V_UNITS + 1:
                        v_norm_of(c, 1)
                        v_stats_of(c, 2)
                        v_low_of(c, 0)
                        v_stats_of(c, 3)
                        v_norm_of(c, 2)
                        v_low_of(c, 1)
                        v_norm_of(c, 3)
                    if n == V_UNITS + 2:
                        v_low_of(c, 2)
                        v_low_of(c, 3)
                    if first and 7 <= n < 7 + MOD_UNITS - MOD_COLS:
                        mod_sum(MOD_COLS + n - 7)
                    if not last and n >= 11 and n < 11 + TILES + 1:
                        j = n - 11
                        if j < TILES:
                            x_stats_of(c + 1, j)
                        if j > 0:
                            x_norm_of(c + 1, j - 1)
                    if not last and IN_UNITS <= n < IN_UNITS + 4:
                        for k in range(2 * (n - IN_UNITS), 2 * (n - IN_UNITS) + 2):
                            h_split(c + 1, k)
                    if n >= IN_UNITS + 4:
                        j = n - IN_UNITS - 4
                        if j == 0:
                            if first:
                                dve.wait_ge(gate_ready, 2)
                                dve.wait_ge(rows_landed, 32)
                            dve.wait_ge(unit_done, c * UNITS + IN_UNITS + 4)
                        z_half(c, j, 0, A)

            run_chunks(dve, chunk)
            z_steps[1].begin(CHUNKS - 1)
            for j in range(TILES):
                dve.wait_ge(unit_done, CHUNKS * UNITS - TILES + j + 1)
                z_half(CHUNKS - 1, j, 1, B)
                if j:
                    z_norm(CHUNKS - 1, j - 1)
            z_norm(CHUNKS - 1, TILES - 1)

        @block.tensor
        def _(pe):
            mm = nc.tensor.matmul

            def product(bank, wh, wl, mh, ml, start, stop):
                mm(bank, wh, mh, start=start, stop=False)
                mm(bank, wh, ml, start=False, stop=False)
                return mm(bank, wl, mh, start=False, stop=stop)

            def token_unit(s, q, tiles, banks, actH, actL, j_order=range(TILES)):
                for j in j_order:
                    cut = slice(j * P, (j + 1) * P)
                    for a, k in enumerate(tiles):
                        row = slice(a * T, (a + 1) * T)
                        last = product(banks[:, j, :], actH[:, k, cut], actL[:, k, cut], wH[:, s, row], wL[:, s, row],
                                       start=(q == 0 and a == 0), stop=(q == 3 and a == 1))
                return last

            def channel_unit(s, bank):
                for k in range(KT):
                    cut = slice(k * P, (k + 1) * P)
                    last = product(bank, wH[:, s, cut], wL[:, s, cut], hH[:, k, :], hL[:, k, :],
                                   start=(k == 0), stop=(k == KT - 1))
                return last

            def turn_x(c, k, bank):
                for j in range(TILES):
                    last = nc.tensor.transpose(B[:, bank, j * P:(j + 1) * P], xn[:, j, k * P:(k + 1) * P], ident[:, :])
                last.then_inc(x_turned, 1)

            def mod_columns(q):
                pe.wait_ge(mod_used, 4 * q + 4)
                wait(pe, mod_ready, q)
                for i in range(4):
                    last = mm(B[:, 3, i:i + 1], macc[:, q, i * P:(i + 1) * P], ones[:, 0:1], start=True, stop=True)
                last.then_inc(mod_summed, 1)

            def small_weights():
                pe.wait_ge(mask_ready, 1)
                pe.wait_ge(mod_ready, V_UNITS)
                for h in range(G):
                    last = nc.tensor.transpose(B[:, 3, h * P:(h + 1) * P], wsN[:, h * P:(h + 1) * P], ident[:, :])
                last.then_inc(wt_turned, 1)
                pe.wait_ge(small_landed, 48)
                pe.wait_ge(wt_ready, 1)
                pe.wait_ge(small_high, 1)
                for h in range(G):
                    cut = slice(h * P, (h + 1) * P)
                    mm(B[:, 3, cut], sgubB[:, cut], wtF[:, cut], start=True, stop=False)
                    last = mm(B[:, 3, cut], ones[0:1, :], bsgu_row[:, cut], start=False, stop=True)
                last.then_inc(e_done, 1)

            def pool_product(c, g):
                pe.wait_ge(p_low, c * G + g + 1)
                pe.wait_ge(v_gelu, (c + 1) * TILES)
                wait(pe, yp_ready, c * G + g - 1)
                product(A[:, g % 2, :], wpH[:, g, :], wpL[:, g, :], pH[:, :], pL[:, :],
                        start=True, stop=True).then_inc(pool_done, 1)

            def sgu_product(c, h):
                pe.wait_ge(v_low, (c + 1) * TILES)
                wait(pe, ys_mixed, c * G + h - 1)
                cut = slice(h * P, (h + 1) * P)
                for j in range(TILES):
                    last = product(A[:, 2 + h % 2, j * P:(j + 1) * P], vH[:, j, cut], vL[:, j, cut],
                                   wtH[:, h, :], wtL[:, h, :], start=True, stop=True)
                last.then_inc(sgu_done, 1)

            pe.wait_ge(vec_landed, 16)
            pe.wait_ge(const_ready, 4)
            nc.tensor.transpose(B[:, 3, 0:V_ROWS], vec_rows[:, :], ident[0:V_ROWS, 0:V_ROWS]).then_inc(vec_turned, 1)
            pe.wait_ge(x_ready, TILES)
            for k in range(3):
                turn_x(0, k, k)
            pe.wait_ge(vec_ready, 1)
            mod_columns(0)
            def more_h(ks):
                for k in ks:
                    pe.wait_ge(h_high, k - 2)
                    turn_x(0, k, k % 3)
            more_h((3, 4))

            banks_of_group = ((0, xa_copied), (1, ga_gated), (2, u_gelu), (3, gb_gated))

            def chunk(c, first, last):
                for n in range(UNITS):
                    s = n % S_SLOTS
                    if not (last and n >= IN_UNITS + 4):
                        pe.wait_ge(w_low, c * UNITS + n + 1)
                    if n < V_UNITS:
                        pe.wait_ge(h_low, c * KT + 2 * n + 2)
                        if n == 0:
                            wait(pe, z_added, c * 2 * TILES - TILES)
                        token_unit(s, n, (2 * n, 2 * n + 1), A, hH, hL).then_inc(unit_done, 1)
                        if first:
                            if n < 3:
                                mod_columns(n + 1)
                                more_h(((5, 6), (7,), ())[n])
                            else:
                                small_weights()
                    elif n < IN_UNITS:
                        g, (bank, freed) = (n - V_UNITS) // 4, banks_of_group[n % 4]
                        if g:
                            pe.wait_ge(freed, c * G + g)
                        elif first:
                            pe.wait_ge(h_high, KT)
                            if bank == 3:
                                pe.wait_ge(small_high, 3)
                        else:
                            pe.wait_ge(z_added, (c - 1) * 2 * TILES + TILES + bank + 1)
                        channel_unit(s, B[:, bank, :]).then_inc(unit_done, 1)
                        if n % 4 == 2:
                            if first and g == 0:
                                pe.wait_ge(small_low, 2)
                            pool_product(c, g)
                            if g:
                                sgu_product(c, g)
                        if n % 4 == 3 and g == 0:
                            sgu_product(c, g)
                        if first and n == IN_UNITS - 2:
                            pe.wait_ge(mod_used, MOD_UNITS)
                            pe.wait_ge(bgate_landed, 16)
                            pe.wait_ge(yp_ready, G - 1)
                            pe.wait_ge(ys_mixed, G - 1)
                            for half in range(2):
                                cut = slice(half * HALF, (half + 1) * HALF)
                                mm(A[:, 2 * half, :], ones[:, :], gateB[:, cut], start=True, stop=False)
                                mm(A[:, 2 * half, :], ones[0:1, :], bgate_row[:, cut], start=False, stop=True)\
                                    .then_inc(gate_summed, 1)
                    else:
                        half, q = (n - IN_UNITS) // 4, (n - IN_UNITS) % 4
                        if half == 0 and not last:
                            for k in (2 * q, 2 * q + 1):
                                if q == 0:
                                    pe.wait_ge(x_ready, (c + 2) * TILES)
                                if k < 4:
                                    pe.wait_ge(banks_of_group[k][1], (c + 1) * G)
                                else:
                                    pe.wait_ge(h_high, (c + 1) * KT + k - 3)
                                turn_x(c + 1, k, k % 4)
                        if half == 0:
                            if q == 0:
                                pe.wait_ge(yp_ready, (c + 1) * G)
                                pe.wait_ge(ys_mixed, (c + 1) * G)
                                if first:
                                    pe.wait_ge(gate_ready, 2)
                            pe.wait_ge(yp_low, c * G + q + 1)
                            pe.wait_ge(ys_low, c * G + q + 1)
                        elif q == 0:
                            if last:
                                for _, freed in banks_of_group:
                                    pe.wait_ge(freed, (c + 1) * G)
                            else:
                                pe.wait_ge(h_high, (c + 2) * KT)
                        if last and half:
                            j = q
                            for i in range(4):
                                if j == 0:
                                    pe.wait_ge(w_low, c * UNITS + IN_UNITS + 4 + i + 1)
                                done = token_unit((IN_UNITS + 4 + i) % S_SLOTS, i, (i, G + i), B, yH, yL, (j,))
                            done.then_inc(unit_done, 1)
                        else:
                            token_unit(s, q, (q, G + q), A if half == 0 else B, yH, yL).then_inc(unit_done, 1)

            run_chunks(pe, chunk)
    return nc


def kernel(x, c, w_ada, b_ada, w_in, w_pool, pool_scale, sgu_ln_g, sgu_ln_b, w_sgu, b_sgu, w_out, ln_g, ln_b):
    import numpy as np
    import concourse.bacc as bacc
    from concourse.bass_utils import run_bass_kernel_spmd

    x, c, w_ada, b_ada, w_in, w_out = (np.asarray(a) for a in (x, c, w_ada, b_ada, w_in, w_out))
    d = x.shape[-1]
    kt, half = d // P, d // 2
    wi = w_in[0].reshape(kt, P, w_in.shape[-1])
    wo = w_out[0].reshape(kt, P, d)
    col_xa, col_ga, col_u, col_v, col_gb = 0, half, 2 * half, 3 * half, 4 * half

    def by_rows(blocks):
        return np.ascontiguousarray(np.transpose(blocks, (1, 0, 2))).reshape(P, -1)

    units = [by_rows(wi[2 * q:2 * q + 2, :, col_v:col_v + T]) for q in range(V_UNITS)]
    for g in range(G):
        units += [by_rows(wi[:, :, col + g * P:col + (g + 1) * P]) for col in (col_xa, col_ga, col_u, col_gb)]
    for h in range(2):
        units += [by_rows(wo[q::G, :, h * half:(h + 1) * half]) for q in range(G)]
    wa = w_ada[0].reshape(kt, P, 3, d)
    mods = []
    for q in range(4):
        pair = wa[:, :, 0:2, 2 * q * P:2 * (q + 1) * P].reshape(kt, P, T)
        mods += [by_rows(pair[2 * r:2 * r + 2]) for r in range(4)]
    mods += [wa[k, :, 2] for k in range(kt)]
    vectors = np.concatenate([c.reshape(-1, P), b_ada[0, :2 * d].reshape(-1, P),
                              np.asarray(pool_scale)[0].reshape(-1, P), np.asarray(sgu_ln_g)[0].reshape(-1, P)])
    arrays = {
        "x": x[0],
        "w_units": np.stack(units),
        "mod_units": np.stack(mods),
        "vectors": vectors,
        "b_gate": b_ada[:, 2 * d:],
        "ln_g": np.asarray(ln_g),
        "ln_b": np.asarray(ln_b),
        "sgu_b": np.asarray(sgu_ln_b).reshape(1, -1),
        "b_sgu": np.asarray(b_sgu).reshape(1, -1),
        "w_pool": np.asarray(w_pool)[0],
        "w_sgu": np.asarray(w_sgu)[0],
    }
    arrays = {name: np.ascontiguousarray(a) for name, a in arrays.items()}
    nc = bacc.Bacc("TRN2", target_bir_lowering=False, num_devices=1)
    handles = [nc.dram_tensor("in_" + name, a.shape, mybir.dt.from_np(a.dtype), kind="ExternalInput").ap()
               for name, a in arrays.items()]
    out = nc.dram_tensor("out", x[0].shape, F32, kind="ExternalOutput").ap()
    hybrid_layer(nc, *handles, out)
    result = run_bass_kernel_spmd(nc, [{"in_" + name: a for name, a in arrays.items()}], core_ids=[0])
    return result.results[0]["out"].reshape(x.shape)
```

```python
from contextlib import ExitStack

import concourse.bass as bass
from concourse import mybir

ALU = mybir.AluOpType
ACT = mybir.ActivationFunctionType
F32 = mybir.dt.float32
F32R = mybir.dt.float32r

P = 128
T = 512
TILES = T // P
G = 4
WINDOWS = (2, 4, 8, 16)
HALO = 16
EPS = 1e-5

V_UNITS = 4
IN_UNITS = V_UNITS + 4 * G
OUT_UNITS = 8
UNITS = IN_UNITS + OUT_UNITS
F_SLOTS = 2
S_SLOTS = 4
AHEAD = 2
MOD_COLS = 16
MOD_UNITS = 24
POOL_AFTER = (7, 10, 14, 18)
SGU_AFTER = (8, 10, 14, 18)
X_STATS_IN = {10: 0, 11: 1, 14: 2, 15: 3}
X_NORM_IN = {11: 0, 14: 1, 15: 2, 18: 3}
GATE_SUMS_IN = {8: (16,), 10: (17,), 12: (18, 19), 14: (20,), 16: (21, 22), 17: (23,)}
GATE_LOADS_IN = {5: 16, 6: 17, 7: 18, 8: 19, 10: 20, 12: 21, 13: 22, 14: 23}
M_SLOTS = 6
GATE_SLOTS = 4
PE_MODS = (0, 1, 4, 8, 12)
DVE_MODS = tuple(m for m in range(MOD_UNITS) if m not in PE_MODS)
V_C, V_SHIFT, V_SCALE, V_PS, V_LG, V_ROWS = 0, 8, 16, 24, 28, 32


class Steps:

    def __init__(self, sem, per_chunk):
        self.sem, self.per_chunk, self.n = sem, per_chunk, per_chunk

    def begin(self, chunk):
        assert self.n == self.per_chunk
        self.chunk, self.n = chunk, 0

    def then(self, eng, instruction):
        self.n += 1
        instruction.then_inc(self.sem, 1)
        eng.wait_ge(self.sem, self.chunk * self.per_chunk + self.n)


def hybrid_layer(nc, x, w_units, mod_units, vectors, b_gate, ln_g, ln_b, sgu_b, b_sgu, w_pool, w_sgu, out):
    D = x.shape[1]
    KT = D // P
    HALF = D // 2
    CHUNKS = x.shape[0] // T
    ALPHA = 2.0 ** 0.25
    assert D == 1024 and KT == 8 and CHUNKS >= 3 and UNITS % S_SLOTS == 0

    x_tiles = x.rearrange("(c j p) d -> c j p d", j=TILES, p=P)
    out_tiles = out.rearrange("(c j p) d -> c j p d", j=TILES, p=P)

    with ExitStack() as ctx:
        def sb(name, shape, dt=F32):
            return ctx.enter_context(nc.sbuf_tensor(name, shape, dt))

        def sem(name):
            return ctx.enter_context(nc.semaphore(name))

        hH, hL = sb("h_high", [P, KT, T], F32R), sb("h_low", [P, KT, T], F32R)
        yH, yL = sb("y_high", [P, KT, T], F32R), sb("y_low", [P, KT, T], F32R)
        wF = sb("w_float", [P, F_SLOTS, 1024])
        wH, wL = sb("w_high", [P, S_SLOTS, 1024], F32R), sb("w_low", [P, S_SLOTS, 1024], F32R)
        xn = sb("x_norm", [P, TILES, D])
        z = sb("z", [P, TILES, D])
        lngB, lnbB, gateB = sb("ln_g_rows", [P, D]), sb("ln_b_rows", [P, D]), sb("gate_rows", [P, D])
        gv = sb("v_gelu", [P, TILES, T])
        vH, vL = sb("v_high", [P, TILES, T], F32R), sb("v_low", [P, TILES, T], F32R)
        wtH, wtL = sb("w_sgu_high", [P, G, P], F32R), sb("w_sgu_low", [P, G, P], F32R)
        wpH, wpL = sb("w_pool_high", [P, G, P], F32R), sb("w_pool_low", [P, G, P], F32R)
        E = sb("sgu_bias", [P, G, P])
        ident, ones = sb("identity", [P, P]), sb("ones", [P, P])
        X = sb("xa", [P, HALO + T])
        S = [sb("sum_a", [P, HALO + T]), sb("sum_b", [P, HALO + T])]
        hF = [s[:, HALO:] for s in S]
        halo = sb("xa_halo", [P, G, HALO])
        pH, pL = sb("pooled_high", [P, T], F32R), sb("pooled_low", [P, T], F32R)
        tanh = sb("tanh", [P, T])
        sga, sgb = sb("gate_a", [P, T]), sb("gate_b", [P, T])
        ug = sb("u_gelu", [P, T])
        mixed = sb("mixed", [P, T])
        yP = sb("y_pool", [P, T])
        vec_rows = sb("vector_rows", [V_ROWS, P])
        cols = sb("vector_cols", [P, V_ROWS])
        ctanh = sb("c_tanh", [P, KT])
        csilu = sb("c_silu", [P, KT])
        modc = sb("mod_cols", [P, KT // 2, 4])
        halfc = sb("half_cols", [P, 2 * G])
        count_inv = sb("count_inv", [P, HALO])
        minus_half = sb("minus_half", [P, G])
        xst, xmv = sb("x_stats", [P, TILES, 2, 6]), sb("x_mean_var", [P, TILES, 2])
        zst, zmv = sb("z_stats", [P, TILES, 2, 6]), sb("z_mean_var", [P, TILES, 2])
        vst, vmv = sb("v_stats", [P, TILES, G, 6]), sb("v_mean_var", [P, TILES, G, 2])
        xve, xrs = sb("x_var_eps", [P, TILES]), sb("x_rstd", [P, TILES])
        zve, zrs = sb("z_var_eps", [P, TILES]), sb("z_rstd", [P, TILES])
        vve, vrs = sb("v_var_eps", [P, TILES, G]), sb("v_rstd", [P, TILES, G])
        spare = sb("spare", [P, 1])
        macc = gv
        wtF, wpF, sgubB, wsN = gateB[:, 0:HALF], sgb, mixed, yP
        bsgu_row, bgate_row = ug[0:1, :], z[0:1, 0, :]

        A = ctx.enter_context(nc.psum_tensor("bank_a", [P, 4, T], F32))
        B = ctx.enter_context(nc.psum_tensor("bank_b", [P, 4, T], F32))

        w_landed = [sem(f"w_landed{i}") for i in range(F_SLOTS)]
        m_landed = [sem(f"m_landed{i}") for i in range(M_SLOTS)]
        xn_landed = [sem(f"xn_landed{j}") for j in range(TILES)]
        z_landed = [sem(f"z_landed{j}") for j in range(TILES)]
        z_stored = [sem(f"z_stored{j}") for j in range(TILES)]
        vec_landed, small_landed, rows_landed = sem("vec_landed"), sem("small_landed"), sem("rows_landed")
        wsgu_landed, bgate_landed = sem("wsgu_landed"), sem("b_gate_landed")
        const_ready, ident_zero, mask_ready = sem("const_ready"), sem("ident_zero"), sem("mask_ready")
        x_rstd, v_rstd, z_rstd = sem("x_rstd_ready"), sem("v_rstd_ready"), sem("z_rstd_ready")
        w_high, w_low = sem("w_high_ready"), sem("w_low_ready")
        unit_done = sem("unit_done")
        vec_turned, vec_ready, c_tanh, c_ready = sem("vec_turned"), sem("vec_ready"), sem("c_tanh_ready"), sem("c_ready")
        mod_multiplied, mod_used = sem("mod_unit_used_by_tensor"), sem("mod_unit_used_by_vector")
        mod_summed, mod_ready = sem("mod_summed"), sem("mod_ready")
        wt_turned, wt_ready, e_done = sem("wt_turned"), sem("wt_ready"), sem("e_done")
        small_high, small_low = sem("small_high"), sem("small_low")
        gate_summed, gate_ready = sem("gate_summed"), sem("gate_ready")
        setup = Steps(sem("setup_steps"), 0)
        x_stats, x_ready, x_turned = sem("x_stats_ready"), sem("x_norm_ready"), sem("x_turned")
        h_float, h_high, h_low = sem("h_float_ready"), sem("h_high_ready"), sem("h_low_ready")
        v_gelu, v_stats, v_norm = sem("v_gelu_ready"), sem("v_stats_ready"), sem("v_norm_ready")
        v_high, v_low = sem("v_high_ready"), sem("v_low_ready")
        xa_copied, pooled, p_high, p_low = sem("xa_copied"), sem("pooled_ready"), sem("p_high_ready"), sem("p_low_ready")
        ga_tanh, ga_gated, gb_tanh, gb_gated = sem("ga_tanh"), sem("ga_gated"), sem("gb_tanh"), sem("gb_gated")
        u_gelu = sem("u_gelu_ready")
        pool_done, sgu_done = sem("pool_product_done"), sem("sgu_product_done")
        yp_ready, yp_high, yp_low = sem("yp_ready"), sem("yp_high_ready"), sem("yp_low_ready")
        ys_mixed, ys_ready, ys_high, ys_low = sem("sgu_mixed"), sem("ys_ready"), sem("ys_high_ready"), sem("ys_low_ready")
        z_added, z_stats, z_ready = sem("z_added"), sem("z_stats_ready"), sem("z_ready")
        pool_steps = Steps(sem("pool_steps"), sum(range(2, 2 + G)) + G)
        v_steps, x_steps = Steps(sem("v_steps"), 2 * TILES), Steps(sem("x_steps"), 2 * TILES)
        z_steps = [Steps(sem("z_first_half_steps"), TILES), Steps(sem("z_second_half_steps"), 4 * TILES)]

        def wait(eng, s, value):
            if not isinstance(value, int) or value > 0:
                eng.wait_ge(s, value)

        def run_chunks(eng, chunk):
            chunk(0, True, False)
            with eng.Fori(1, CHUNKS - 1) as c:
                chunk(c, False, False)
            chunk(CHUNKS - 1, False, True)

        def m_sem(m):
            return m % M_SLOTS if m < MOD_COLS else m % GATE_SLOTS

        def m_slot(m):
            n = m_sem(m)
            return z[:, n, :] if n < TILES else (lngB, lnbB)[n - TILES][:, :]

        def m_wait(eng, m):
            nth = sum(1 for i in range(m + 1) if m_sem(i) == m_sem(m))
            eng.wait_ge(m_landed[m_sem(m)], nth * 16)

        block = ctx.enter_context(nc.Block())

        @block.sync
        def _(sp):
            def load_w(c, n):
                wait(sp, w_low, c * UNITS + n - F_SLOTS + 1)
                sp.dma_start(wF[:, n % F_SLOTS, :], w_units[n % UNITS]).then_inc(w_landed[n % F_SLOTS], 16)

            def load_m(m):
                before = m - M_SLOTS
                if m == MOD_COLS:
                    before = MOD_COLS - 1
                elif m > MOD_COLS:
                    before = m - GATE_SLOTS
                if before in PE_MODS:
                    sp.wait_ge(mod_multiplied, PE_MODS.index(before) + 1)
                elif before > 0:
                    sp.wait_ge(mod_used, DVE_MODS.index(before) + 1)
                sp.dma_start(m_slot(m), mod_units[m]).then_inc(m_landed[m_sem(m)], 16)

            sp.dma_start(vec_rows[:, :], vectors).then_inc(vec_landed, 16)
            for j in range(TILES):
                sp.dma_start(xn[:, j, :], x_tiles[0, j]).then_inc(xn_landed[j], 16)
            for q in range(V_UNITS):
                for m in range(4 * q, 4 * q + 4):
                    load_m(m)
                load_w(0, q)
                if q == V_UNITS - 1:
                    sp.dma_start(wsN[:, :].rearrange("p (h s) -> p h s", h=G),
                                 w_sgu.rearrange("h t s -> t h s")).then_inc(wsgu_landed, 16)
                    sp.dma_start(wpF[:, :].rearrange("p (g d) -> p g d", g=G),
                                 w_pool.rearrange("g c d -> c g d")).then_inc(small_landed, 16)
                    sp.dma_start(sgubB[:, :], sgu_b.broadcast_to([P, G * P])).then_inc(small_landed, 16)
                    sp.dma_start(bsgu_row, b_sgu).then_inc(small_landed, 16)

            def chunk(c, first, last):
                for n in range(UNITS):
                    if n + 2 * AHEAD < UNITS or not last:
                        load_w(c, n + 2 * AHEAD)
                    if first and n == 7:
                        sp.dma_start(lngB[:, :], ln_g.broadcast_to([P, D])).then_inc(rows_landed, 16)
                        sp.dma_start(lnbB[:, :], ln_b.broadcast_to([P, D])).then_inc(rows_landed, 16)
                    if first and n in GATE_LOADS_IN:
                        load_m(GATE_LOADS_IN[n])
                    if first and n == 16:
                        sp.wait_ge(mod_used, DVE_MODS.index(MOD_UNITS - GATE_SLOTS) + 1)
                        sp.dma_start(bgate_row, b_gate).then_inc(bgate_landed, 16)
                    if not first and 2 <= n < 2 + TILES:
                        j = n - 2
                        sp.wait_ge(z_ready, (c - 1) * TILES + j + 1)
                        sp.dma_start(out_tiles[c - 1, j], z[:, j, :]).then_inc(z_stored[j], 16)
                    if not last and 6 <= n < 6 + TILES:
                        j = n - 6
                        sp.wait_ge(x_turned, (c + 1) * KT)
                        sp.dma_start(xn[:, j, :], x_tiles[c + 1, j]).then_inc(xn_landed[j], 16)
                    if 17 <= n < 17 + TILES:
                        j = n - 17
                        if first:
                            sp.wait_ge(mod_used, len(DVE_MODS))
                            sp.wait_ge(gate_summed, 2)
                        else:
                            sp.wait_ge(z_stored[j], c * 16)
                        sp.dma_start(z[:, j, :], x_tiles[c, j]).then_inc(z_landed[j], 16)

            run_chunks(sp, chunk)
            for j in range(TILES):
                sp.wait_ge(z_ready, (CHUNKS - 1) * TILES + j + 1)
                sp.dma_start(out_tiles[CHUNKS - 1, j], z[:, j, :]).then_inc(z_stored[j], 16)
            for j in range(TILES):
                sp.wait_ge(z_stored[j], CHUNKS * 16)

        @block.gpsimd
        def _(pool):
            nc.gpsimd.memset(ident[:, :], 0.0).then_inc(ident_zero, 1)
            nc.gpsimd.memset(ones[:, :], 1.0).then_inc(const_ready, 1)
            nc.gpsimd.memset(minus_half[:, :], -0.5).then_inc(const_ready, 1)
            nc.gpsimd.memset(halo[:, :, :], 0.0).then_inc(const_ready, 1)
            pool.wait_ge(ident_zero, 1)
            nc.gpsimd.affine_select(out=ident[:, :], in_=ident[:, :], compare_op=ALU.not_equal, fill=1.0, base=0,
                                    pattern=[[-1, P]], channel_multiplier=1).then_inc(const_ready, 1)

            def rstd(ready, var_eps, rstd_out, exponent):
                nc.gpsimd.tensor_tensor(rstd_out, var_eps, exponent, ALU.pow).then_inc(ready, 1)

            def x_rstds(c, j):
                pool.wait_ge(x_stats, c * TILES + j + 1)
                rstd(x_rstd, xve[:, j:j + 1], xrs[:, j:j + 1], minus_half[:, 0:1])

            pool.wait_ge(const_ready, 4)
            for j in range(TILES):
                x_rstds(0, j)
            for t in range(HALO):
                nc.gpsimd.memset(count_inv[:, t:t + 1], 1.0 / (t + 1)).then_inc(const_ready, 1)
            for n in range(V_UNITS):
                pool.wait_ge(w_high, n + 1)
                nc.gpsimd.tensor_tensor(wL[:, n, :], wF[:, n % F_SLOTS, :], wH[:, n, :].bitcast(F32), ALU.subtract)\
                    .then_inc(w_low, 1)
            pool.wait_ge(wsgu_landed, 16)
            ws = wsN[:, :].rearrange("p (h s) -> p h s", h=G)
            nc.gpsimd.affine_select(out=ws, in_=ws, compare_op=ALU.is_ge, fill=0.0, base=0,
                                    pattern=[[0, G], [-1, P]], channel_multiplier=1).then_inc(mask_ready, 1)

            def z_rstds(c, j):
                pool.wait_ge(z_stats, c * TILES + j + 1)
                rstd(z_rstd, zve[:, j:j + 1], zrs[:, j:j + 1], minus_half[:, 0:1])

            def chunk(c, first, last):
                if not first:
                    for j in range(TILES):
                        z_rstds(c - 1, j)
                for j in range(TILES):
                    pool.wait_ge(v_stats, c * TILES + j + 1)
                    rstd(v_rstd, vve[:, j, :], vrs[:, j, :], minus_half[:, :])
                if not last:
                    for j in range(TILES):
                        x_rstds(c + 1, j)

            run_chunks(pool, chunk)
            for j in range(TILES):
                z_rstds(CHUNKS - 1, j)

        @block.scalar
        def _(act):
            def split_high(c, n):
                wait(act, unit_done, c * UNITS + n - S_SLOTS + 1)
                act.wait_ge(w_landed[n % F_SLOTS], (c * (UNITS // F_SLOTS) + n // F_SLOTS + 1) * 16)
                nc.scalar.activation(wH[:, n % S_SLOTS, :], wF[:, n % F_SLOTS, :], ACT.Copy).then_inc(w_high, 1)

            def h_evacuate(c, k):
                act.wait_ge(x_turned, c * KT + k + 1)
                wait(act, h_low, c * KT + k - 1)
                bank = B[:, k % 3 if isinstance(c, int) and c == 0 else k % 4, :]
                shift, scale = modc[:, k // 2, k % 2:k % 2 + 1], modc[:, k // 2, 2 + k % 2:3 + k % 2]
                nc.scalar.activation(hF[k % 2], bank, ACT.Identity, bias=shift, scale=scale).then_inc(h_float, 1)
                nc.scalar.activation(hH[:, k, :], bank, ACT.Identity, bias=shift, scale=scale).then_inc(h_high, 1)

            act.wait_ge(vec_turned, 1)
            nc.scalar.activation(cols[:, :], B[:, 3, 0:V_ROWS], ACT.Copy).then_inc(vec_ready, 1)
            act.wait_ge(vec_ready, 1)
            nc.scalar.activation(ctanh[:, :], cols[:, V_C:V_C + KT], ACT.Tanh, scale=0.5).then_inc(c_tanh, 1)
            for q in range(V_UNITS):
                split_high(0, q)
                act.wait_ge(mod_ready, q + 1)
                h_evacuate(0, 2 * q)
                h_evacuate(0, 2 * q + 1)
            def small_weights():
                act.wait_ge(wt_turned, 1)
                nc.scalar.activation(wtF, B[:, 3, :], ACT.Copy).then_inc(wt_ready, 1)
                nc.scalar.activation(wtH[:, :, :].rearrange("p h t -> p (h t)"), B[:, 3, :], ACT.Copy)\
                    .then_inc(small_high, 1)
                act.wait_ge(small_landed, 48)
                nc.scalar.activation(wpH[:, :, :].rearrange("p g d -> p (g d)"), wpF[:, :], ACT.Copy)\
                    .then_inc(small_high, 1)

            def sgu_bias():
                act.wait_ge(e_done, 1)
                nc.scalar.activation(E[:, :, :].rearrange("p h t -> p (h t)"), B[:, 3, :], ACT.Copy, scale=0.5)\
                    .then_inc(small_high, 1)

            def chunk(c, first, last):
                for n in range(UNITS):
                    if (n + AHEAD < UNITS or not last) and not (first and n + AHEAD < V_UNITS):
                        split_high(c, n + AHEAD)
                    if n == V_UNITS:
                        act.wait_ge(unit_done, c * UNITS + V_UNITS)
                        for j in range(TILES):
                            nc.scalar.activation(gv[:, j, :], A[:, j, :], ACT.Gelu).then_inc(v_gelu, 1)
                    g, step = (n - V_UNITS - 1) // 4, (n - V_UNITS - 1) % 4
                    if n > V_UNITS and g < G:
                        act.wait_ge(unit_done, c * UNITS + n)
                        if step == 0:
                            wait(act, pooled, c * G + g)
                            nc.scalar.activation(X[:, HALO:], B[:, 0, :], ACT.Copy).then_inc(xa_copied, 1)
                        if step == 1:
                            nc.scalar.activation(tanh[:, :], B[:, 1, :], ACT.Tanh, scale=0.5).then_inc(ga_tanh, 1)
                            act.wait_ge(pooled, c * G + g + 1)
                            nc.scalar.activation(pH[:, :], S[(g + 1) % 2][:, HALO:], ACT.Copy).then_inc(p_high, 1)
                        if step == 2:
                            wait(act, ys_mixed, c * G + g)
                            nc.scalar.activation(ug[:, :], B[:, 2, :], ACT.Gelu).then_inc(u_gelu, 1)
                        if step == 3:
                            act.wait_ge(ga_gated, c * G + g + 1)
                            nc.scalar.activation(tanh[:, :], B[:, 3, :], ACT.Tanh, scale=0.5).then_inc(gb_tanh, 1)
                    for g in range(G):
                        if n == POOL_AFTER[g] + 2:
                            act.wait_ge(yp_ready, c * G + g + 1)
                            nc.scalar.activation(yH[:, g, :], yP[:, :], ACT.Copy).then_inc(yp_high, 1)
                        if n == SGU_AFTER[g] + 2:
                            act.wait_ge(ys_ready, c * G + g + 1)
                            nc.scalar.activation(yH[:, G + g, :], mixed[:, :], ACT.Copy).then_inc(ys_high, 1)
                    if first and n == V_UNITS + 1:
                        small_weights()
                    if first and n == V_UNITS + 2:
                        sgu_bias()
                    if V_UNITS < n <= V_UNITS + 2:
                        for j in range(2 * (n - V_UNITS - 1), 2 * (n - V_UNITS)):
                            act.wait_ge(v_norm, c * TILES + j + 1)
                            nc.scalar.activation(vH[:, j, :], gv[:, j, :], ACT.Copy).then_inc(v_high, 1)
                    if first and n == IN_UNITS - 1:
                        act.wait_ge(gate_summed, 2)
                        for half in range(2):
                            nc.scalar.activation(gateB[:, half * HALF:(half + 1) * HALF], A[:, 2 * half, :], ACT.Copy)\
                                .then_inc(gate_ready, 1)
                    if not last and IN_UNITS <= n < IN_UNITS + 4:
                        for k in range(2 * (n - IN_UNITS), 2 * (n - IN_UNITS) + 2):
                            h_evacuate(c + 1, k)

            run_chunks(act, chunk)

        @block.vector
        def _(dve):
            vec = nc.vector

            def split_low(c, n):
                dve.wait_ge(w_high, c * UNITS + n + 1)
                vec.tensor_tensor(wL[:, n % S_SLOTS, :], wF[:, n % F_SLOTS, :],
                                  wH[:, n % S_SLOTS, :].bitcast(F32), ALU.subtract).then_inc(w_low, 1)

            def h_split(c, k):
                dve.wait_ge(h_high, c * KT + k + 1)
                vec.tensor_tensor(hL[:, k, :], hF[k % 2], hH[:, k, :].bitcast(F32), ALU.subtract).then_inc(h_low, 1)

            def aggregate(steps, out_stats, in_stats, last_stats):
                steps.then(dve, last_stats)
                vec.memset(spare[:, :], 0.0)
                for o, i in zip(out_stats, in_stats):
                    last = vec.bn_aggr(o, i)
                steps.then(dve, last)

            def x_stats_of(c, j):
                dve.wait_ge(xn_landed[j], (c + 1) * 16)
                for h in range(2):
                    last = vec.bn_stats(xst[:, j, h, :], xn[:, j, h * HALF:(h + 1) * HALF])
                aggregate(x_steps, [xmv[:, j, :]], [xst[:, j, :, :].rearrange("p a b -> p (a b)")], last)
                vec.tensor_scalar(xve[:, j:j + 1], xmv[:, j, 1:2], EPS, None, ALU.add).then_inc(x_stats, 1)

            def x_norm_of(c, j):
                dve.wait_ge(x_rstd, c * TILES + j + 1)
                vec.tensor_scalar(xn[:, j, :], xn[:, j, :], xmv[:, j, 0:1], xrs[:, j:j + 1],
                                  ALU.subtract, ALU.mult).then_inc(x_ready, 1)

            def mod_sum(m):
                m_wait(dve, m)
                unit = m_slot(m)
                if m < MOD_COLS:
                    parts = [(macc[:, m // 4, :], unit[:, a * T:(a + 1) * T], 2 * (m % 4) + a) for a in range(2)]
                else:
                    parts = [(gateB[:, :], unit, m - MOD_COLS)]
                for n, (acc, rows, k) in enumerate(parts):
                    c_col = csilu[:, k:k + 1]
                    if (m - 1 in PE_MODS or m == MOD_COLS) and n == 0:
                        ins = vec.tensor_scalar(acc, rows, c_col, None, ALU.mult)
                    else:
                        ins = vec.scalar_tensor_tensor(out=acc, in0=rows, scalar=c_col, in1=acc,
                                                       op0=ALU.mult, op1=ALU.add)
                    if n < len(parts) - 1:
                        setup.then(dve, ins)
                ins.then_inc(mod_used, 1)
                dve.wait_ge(mod_used, DVE_MODS.index(m) + 1)

            setup.begin(0)
            x_steps.begin(0)
            for j in range(TILES):
                x_stats_of(0, j)
                if j == 0:
                    dve.wait_ge(vec_ready, 1)
                    dve.wait_ge(c_tanh, 1)
                    setup.then(dve, vec.scalar_tensor_tensor(out=csilu[:, :], in0=ctanh[:, :], scalar=1.0,
                                                             in1=cols[:, V_C:V_C + KT], op0=ALU.add, op1=ALU.mult))
                    vec.tensor_scalar(csilu[:, :], csilu[:, :], 0.5, None, ALU.mult).then_inc(c_ready, 1)
                    vec.tensor_scalar(halfc[:, :], cols[:, V_PS:V_PS + 2 * G], 0.5, None, ALU.mult).then_inc(c_ready, 1)
                    vec.tensor_scalar(cols[:, V_SCALE:V_SCALE + KT], cols[:, V_SCALE:V_SCALE + KT], 1.0, None,
                                      ALU.add).then_inc(c_ready, 1)
                else:
                    x_norm_of(0, j - 1)
            x_norm_of(0, TILES - 1)
            dve.wait_ge(c_ready, 3)
            for q in range(V_UNITS):
                units = [m for m in DVE_MODS if m // 4 == q]
                for n, m in enumerate(units):
                    mod_sum(m)
                    if q and n != 1:
                        h_split(0, 2 * q - 2 + n // 2)
                dve.wait_ge(mod_summed, q + 1)
                bias = cols[:, V_SHIFT:V_SHIFT + 2 * KT].rearrange("p (s k) -> p s k", s=2)[:, :, 2 * q:2 * q + 2]
                vec.tensor_tensor(modc[:, q, :].rearrange("p (s k) -> p s k", s=2),
                                  B[:, 3, 0:4].rearrange("p (s k) -> p s k", s=2), bias, ALU.add).then_inc(mod_ready, 1)
            h_split(0, KT - 2)
            h_split(0, KT - 1)

            dve.wait_ge(w_low, V_UNITS)

            def small_weights():
                dve.wait_ge(small_high, 2)
                vec.tensor_tensor(wtL[:, :, :].rearrange("p h t -> p (h t)"), wtF,
                                  wtH[:, :, :].rearrange("p h t -> p (h t)").bitcast(F32), ALU.subtract)\
                    .then_inc(small_low, 1)
                vec.tensor_tensor(wpL[:, :, :].rearrange("p g d -> p (g d)"), wpF[:, :],
                                  wpH[:, :, :].rearrange("p g d -> p (g d)").bitcast(F32), ALU.subtract)\
                    .then_inc(small_low, 1)

            def pooling(c, g, first):
                w = WINDOWS[g]
                if g == 0 and first:
                    dve.wait_ge(const_ready, 4 + HALO)
                wait(dve, p_low, c * G + g)
                wait(dve, h_low, (c + 1) * KT)
                dve.wait_ge(xa_copied, c * G + g + 1)
                pool_steps.then(dve, vec.tensor_copy(X[:, 0:HALO], halo[:, g, :]))
                src = X
                for level in range(g + 1):
                    shift = 1 << level
                    lo = HALO - (w - 2 * shift)
                    dst = S[level % 2]
                    pool_steps.then(dve, vec.tensor_tensor(dst[:, lo:], src[:, lo:],
                                                           src[:, lo - shift:HALO + T - shift], ALU.add))
                    src = dst
                dst = S[(g + 1) % 2]
                vec.tensor_copy(halo[:, g, :], X[:, T:])
                mean = vec.scalar_tensor_tensor(out=dst[:, HALO:], in0=src[:, HALO:], scalar=1.0 / w,
                                                in1=X[:, HALO:], op0=ALU.mult, op1=ALU.subtract)
                if first:
                    head = slice(HALO, HALO + w - 1)
                    setup.then(dve, mean)
                    setup.then(dve, vec.tensor_tensor(dst[:, head], src[:, head], count_inv[:, 0:w - 1], ALU.mult))
                    mean = vec.tensor_tensor(dst[:, head], dst[:, head], X[:, head], ALU.subtract)
                mean.then_inc(pooled, 1)

            def pooled_low(c, g):
                dve.wait_ge(p_high, c * G + g + 1)
                vec.tensor_tensor(pL[:, :], S[(g + 1) % 2][:, HALO:], pH[:, :].bitcast(F32), ALU.subtract).then_inc(p_low, 1)

            def gate(tanh_ready, gated, out_t, bank, value):
                dve.wait_ge(tanh_ready, value)
                vec.scalar_tensor_tensor(out=out_t[:, :], in0=tanh[:, :], scalar=1.0, in1=B[:, bank, :],
                                         op0=ALU.add, op1=ALU.mult).then_inc(gated, 1)

            def y_pool(c, g):
                dve.wait_ge(pool_done, c * G + g + 1)
                wait(dve, yp_low, c * G + g)
                dve.wait_ge(ga_gated, c * G + g + 1)
                vec.scalar_tensor_tensor(out=yP[:, :], in0=A[:, g % 2, :], scalar=halfc[:, g:g + 1], in1=sga[:, :],
                                         op0=ALU.mult, op1=ALU.mult).then_inc(yp_ready, 1)

            def mix(c, g, first):
                dve.wait_ge(sgu_done, c * G + g + 1)
                wait(dve, ys_low, c * G + g)
                if first and g == 0:
                    dve.wait_ge(small_high, 3)
                tiles = "p (j t) -> p j t"
                bias = E[:, g:g + 1, :].broadcast_to([P, TILES, P])
                pool_steps.then(dve, vec.scalar_tensor_tensor(
                    out=mixed[:, :].rearrange(tiles, j=TILES), in0=A[:, 2 + g % 2, :].rearrange(tiles, j=TILES),
                    scalar=halfc[:, G + g:G + g + 1], in1=bias, op0=ALU.mult, op1=ALU.add))
                dve.wait_ge(u_gelu, c * G + g + 1)
                vec.tensor_tensor(mixed[:, :], mixed[:, :], ug[:, :], ALU.mult).then_inc(ys_mixed, 1)

            def y_low(c, g, high, low, row, src):
                dve.wait_ge(high, c * G + g + 1)
                vec.tensor_tensor(yL[:, row, :], src[:, :], yH[:, row, :].bitcast(F32), ALU.subtract).then_inc(low, 1)

            def v_stats_of(c, j):
                dve.wait_ge(v_gelu, c * TILES + j + 1)
                for h in range(G):
                    last = vec.bn_stats(vst[:, j, h, :], gv[:, j, h * P:(h + 1) * P])
                aggregate(v_steps, [vmv[:, j, h, :] for h in range(G)], [vst[:, j, h, :] for h in range(G)], last)
                vec.tensor_scalar(vve[:, j, :], vmv[:, j, :, 1], EPS, None, ALU.add).then_inc(v_stats, 1)

            def v_norm_of(c, j):
                dve.wait_ge(v_rstd, c * TILES + j + 1)
                for h in range(G):
                    head = gv[:, j, h * P:(h + 1) * P]
                    last = vec.tensor_scalar(head, head, vmv[:, j, h, 0:1], vrs[:, j, h:h + 1], ALU.subtract, ALU.mult)
                last.then_inc(v_norm, 1)

            def v_low_of(c, j):
                dve.wait_ge(v_high, c * TILES + j + 1)
                vec.tensor_tensor(vL[:, j, :], gv[:, j, :], vH[:, j, :].bitcast(F32), ALU.subtract).then_inc(v_low, 1)

            def z_half(c, j, half, bank):
                cut = slice(half * HALF, (half + 1) * HALF)
                if half == 0:
                    dve.wait_ge(z_landed[j], (c + 1) * 16)
                product = vec.tensor_tensor(tanh[:, :], bank[:, j, :], gateB[:, cut], ALU.mult)
                product.then_inc(z_added, 1)
                dve.wait_ge(z_added, c * 2 * TILES + half * TILES + j + 1)
                z_steps[half].then(dve, vec.scalar_tensor_tensor(out=z[:, j, cut], in0=z[:, j, cut], scalar=ALPHA,
                                                                 in1=tanh[:, :], op0=ALU.mult, op1=ALU.add))
                stats = vec.bn_stats(zst[:, j, half, :], z[:, j, cut])
                if half:
                    aggregate(z_steps[1], [zmv[:, j, :]], [zst[:, j, :, :].rearrange("p a b -> p (a b)")], stats)
                    vec.tensor_scalar(zve[:, j:j + 1], zmv[:, j, 1:2], EPS, None, ALU.add).then_inc(z_stats, 1)

            def z_norm(c, j):
                dve.wait_ge(z_rstd, c * TILES + j + 1)
                z_steps[1].then(dve, vec.scalar_tensor_tensor(out=z[:, j, :], in0=z[:, j, :], scalar=zmv[:, j, 0:1],
                                                              in1=lngB[:, :], op0=ALU.subtract, op1=ALU.mult))
                vec.scalar_tensor_tensor(out=z[:, j, :], in0=z[:, j, :], scalar=zrs[:, j:j + 1], in1=lnbB[:, :],
                                         op0=ALU.mult, op1=ALU.add).then_inc(z_ready, 1)

            def chunk(c, first, last):
                for steps in (pool_steps, v_steps, z_steps[0]):
                    steps.begin(c)
                if not first:
                    z_steps[1].begin(c - 1)
                if not last:
                    x_steps.begin(c + 1)
                for n in range(UNITS):
                    if (n + AHEAD < UNITS or not last) and not (first and n + AHEAD < V_UNITS):
                        split_low(c, n + AHEAD)
                    if not first and n < TILES + 1:
                        if n < TILES:
                            if n == 0:
                                dve.wait_ge(unit_done, c * UNITS)
                            z_half(c - 1, n, 1, B)
                        if n > 0:
                            z_norm(c - 1, n - 1)
                    if n == V_UNITS:
                        v_stats_of(c, 0)
                        v_stats_of(c, 1)
                        v_norm_of(c, 0)
                    g, step = (n - V_UNITS - 1) // 4, (n - V_UNITS - 1) % 4
                    if n > V_UNITS and g < G:
                        if step == 0:
                            pooling(c, g, first)
                        if step == 1:
                            pooled_low(c, g)
                            gate(ga_tanh, ga_gated, sga, 1, c * G + g + 1)
                        if step == 3:
                            if first and g == 0:
                                dve.wait_ge(small_low, 2)
                            gate(gb_tanh, gb_gated, sgb, 3, c * G + g + 1)
                    if first and n == V_UNITS + 2:
                        small_weights()
                    for g in range(G):
                        if n == POOL_AFTER[g] + 1:
                            y_pool(c, g)
                        if n == SGU_AFTER[g] + 1:
                            mix(c, g, first)
                        if n == SGU_AFTER[g] + 2:
                            dve.wait_ge(ys_mixed, c * G + g + 1)
                            dve.wait_ge(gb_gated, c * G + g + 1)
                            vec.tensor_tensor(mixed[:, :], mixed[:, :], sgb[:, :], ALU.mult).then_inc(ys_ready, 1)
                        if n == POOL_AFTER[g] + 2:
                            y_low(c, g, yp_high, yp_low, g, yP)
                        if n == SGU_AFTER[g] + 2:
                            y_low(c, g, ys_high, ys_low, G + g, mixed)
                    if n == V_UNITS + 1:
                        v_norm_of(c, 1)
                        v_stats_of(c, 2)
                        v_low_of(c, 0)
                        v_stats_of(c, 3)
                        v_norm_of(c, 2)
                        v_low_of(c, 1)
                        v_norm_of(c, 3)
                    if n == V_UNITS + 2:
                        v_low_of(c, 2)
                        v_low_of(c, 3)
                    if first:
                        for m in GATE_SUMS_IN.get(n, ()):
                            if m == MOD_COLS:
                                dve.wait_ge(e_done, 1)
                            mod_sum(m)
                    if not last and n in X_NORM_IN:
                        x_norm_of(c + 1, X_NORM_IN[n])
                    if not last and n in X_STATS_IN:
                        x_stats_of(c + 1, X_STATS_IN[n])
                    if not last and IN_UNITS <= n < IN_UNITS + 4:
                        for k in range(2 * (n - IN_UNITS), 2 * (n - IN_UNITS) + 2):
                            h_split(c + 1, k)
                    if n >= IN_UNITS + 4:
                        j = n - IN_UNITS - 4
                        if j == 0:
                            if first:
                                dve.wait_ge(gate_ready, 2)
                                dve.wait_ge(rows_landed, 32)
                            dve.wait_ge(unit_done, c * UNITS + IN_UNITS + 4)
                        z_half(c, j, 0, A)

            run_chunks(dve, chunk)
            z_steps[1].begin(CHUNKS - 1)
            for j in range(TILES):
                dve.wait_ge(unit_done, CHUNKS * UNITS - TILES + j + 1)
                z_half(CHUNKS - 1, j, 1, B)
                if j:
                    z_norm(CHUNKS - 1, j - 1)
            z_norm(CHUNKS - 1, TILES - 1)

        @block.tensor
        def _(pe):
            mm = nc.tensor.matmul

            def product(bank, wh, wl, mh, ml, start, stop):
                mm(bank, wh, mh, start=start, stop=False)
                mm(bank, wh, ml, start=False, stop=False)
                return mm(bank, wl, mh, start=False, stop=stop)

            def token_unit(s, q, tiles, banks, actH, actL, j_order=range(TILES)):
                for j in j_order:
                    cut = slice(j * P, (j + 1) * P)
                    for a, k in enumerate(tiles):
                        row = slice(a * T, (a + 1) * T)
                        last = product(banks[:, j, :], actH[:, k, cut], actL[:, k, cut], wH[:, s, row], wL[:, s, row],
                                       start=(q == 0 and a == 0), stop=(q == 3 and a == 1))
                return last

            def channel_unit(s, bank):
                for k in range(KT):
                    cut = slice(k * P, (k + 1) * P)
                    last = product(bank, wH[:, s, cut], wL[:, s, cut], hH[:, k, :], hL[:, k, :],
                                   start=(k == 0), stop=(k == KT - 1))
                return last

            def turn_x(c, k, bank):
                for j in range(TILES):
                    last = nc.tensor.transpose(B[:, bank, j * P:(j + 1) * P], xn[:, j, k * P:(k + 1) * P], ident[:, :])
                last.then_inc(x_turned, 1)

            def mod_columns(q):
                wait(pe, mod_ready, q)
                if q == 0:
                    pe.wait_ge(vec_ready, 1)
                    pe.wait_ge(c_ready, 1)
                for m in PE_MODS:
                    if m // 4 == q:
                        m_wait(pe, m)
                        for k in (2 * (m % 4), 2 * (m % 4) + 1):
                            for i in range(4):
                                col = (k % 2) * T + i * P
                                last = mm(B[:, 3, i:i + 1], m_slot(m)[:, col:col + P], csilu[:, k:k + 1],
                                          start=(k == 0 and i == 0), stop=False, skip_group_check=True)
                        last.then_inc(mod_multiplied, 1)
                pe.wait_ge(mod_used, max(n for n, m in enumerate(DVE_MODS) if m // 4 == q) + 1)
                for i in range(4):
                    last = mm(B[:, 3, i:i + 1], macc[:, q, i * P:(i + 1) * P], ones[:, 0:1], start=False, stop=True,
                              skip_group_check=True)
                last.then_inc(mod_summed, 1)

            def turn_w_sgu():
                pe.wait_ge(mask_ready, 1)
                pe.wait_ge(mod_ready, V_UNITS)
                for h in range(G):
                    last = nc.tensor.transpose(B[:, 3, h * P:(h + 1) * P], wsN[:, h * P:(h + 1) * P], ident[:, :])
                last.then_inc(wt_turned, 1)

            def sgu_bias():
                pe.wait_ge(small_landed, 48)
                pe.wait_ge(wt_ready, 1)
                pe.wait_ge(small_high, 1)
                for h in range(G):
                    cut = slice(h * P, (h + 1) * P)
                    mm(B[:, 3, cut], sgubB[:, cut], wtF[:, cut], start=True, stop=False)
                    last = mm(B[:, 3, cut], ones[0:1, :], bsgu_row[:, cut], start=False, stop=True)
                last.then_inc(e_done, 1)

            def pool_product(c, g):
                pe.wait_ge(p_low, c * G + g + 1)
                pe.wait_ge(v_gelu, (c + 1) * TILES)
                wait(pe, yp_ready, c * G + g - 1)
                product(A[:, g % 2, :], wpH[:, g, :], wpL[:, g, :], pH[:, :], pL[:, :],
                        start=True, stop=True).then_inc(pool_done, 1)

            def sgu_product(c, h):
                pe.wait_ge(v_low, (c + 1) * TILES)
                wait(pe, ys_mixed, c * G + h - 1)
                cut = slice(h * P, (h + 1) * P)
                for j in range(TILES):
                    last = product(A[:, 2 + h % 2, j * P:(j + 1) * P], vH[:, j, cut], vL[:, j, cut],
                                   wtH[:, h, :], wtL[:, h, :], start=True, stop=True)
                last.then_inc(sgu_done, 1)

            pe.wait_ge(vec_landed, 16)
            pe.wait_ge(const_ready, 4)
            nc.tensor.transpose(B[:, 3, 0:V_ROWS], vec_rows[:, :], ident[0:V_ROWS, 0:V_ROWS]).then_inc(vec_turned, 1)
            mod_columns(0)
            pe.wait_ge(x_ready, TILES)
            for k in range(3):
                turn_x(0, k, k)
            def more_h(ks):
                for k in ks:
                    pe.wait_ge(h_high, k - 2)
                    turn_x(0, k, k % 3)
            more_h((3, 4))
            mod_columns(1)

            banks_of_group = ((0, xa_copied), (1, ga_gated), (2, u_gelu), (3, gb_gated))

            def chunk(c, first, last):
                for n in range(UNITS):
                    s = n % S_SLOTS
                    if not (last and n >= IN_UNITS + 4):
                        pe.wait_ge(w_low, c * UNITS + n + 1)
                    if n < V_UNITS:
                        pe.wait_ge(h_low, c * KT + 2 * n + 2)
                        if n == 0:
                            wait(pe, z_added, c * 2 * TILES - TILES)
                        token_unit(s, n, (2 * n, 2 * n + 1), A, hH, hL).then_inc(unit_done, 1)
                        if first:
                            more_h(((5, 6), (7,), (), ())[n])
                            if n < V_UNITS - 2:
                                mod_columns(n + 2)
                    elif n < IN_UNITS:
                        g, (bank, freed) = (n - V_UNITS) // 4, banks_of_group[n % 4]
                        if g:
                            pe.wait_ge(freed, c * G + g)
                        elif first:
                            pe.wait_ge(h_high, KT)
                            if bank == 3:
                                pe.wait_ge(small_high, 3)
                        else:
                            pe.wait_ge(z_added, (c - 1) * 2 * TILES + TILES + bank + 1)
                        channel_unit(s, B[:, bank, :]).then_inc(unit_done, 1)
                        if first and n == V_UNITS:
                            turn_w_sgu()
                        if first and n == V_UNITS + 1:
                            sgu_bias()
                        if n in POOL_AFTER:
                            if first and n == POOL_AFTER[0]:
                                pe.wait_ge(small_low, 2)
                            pool_product(c, POOL_AFTER.index(n))
                        if n in SGU_AFTER:
                            sgu_product(c, SGU_AFTER.index(n))
                        if first and n == IN_UNITS - 2:
                            pe.wait_ge(mod_used, len(DVE_MODS))
                            pe.wait_ge(bgate_landed, 16)
                            pe.wait_ge(yp_ready, G - 1)
                            pe.wait_ge(ys_mixed, G - 1)
                            for half in range(2):
                                cut = slice(half * HALF, (half + 1) * HALF)
                                mm(A[:, 2 * half, :], ones[:, :], gateB[:, cut], start=True, stop=False)
                                mm(A[:, 2 * half, :], ones[0:1, :], bgate_row[:, cut], start=False, stop=True)\
                                    .then_inc(gate_summed, 1)
                    else:
                        half, q = (n - IN_UNITS) // 4, (n - IN_UNITS) % 4
                        if half == 0 and not last:
                            for k in (2 * q, 2 * q + 1):
                                if q == 0:
                                    pe.wait_ge(x_ready, (c + 2) * TILES)
                                if k < 4:
                                    pe.wait_ge(banks_of_group[k][1], (c + 1) * G)
                                else:
                                    pe.wait_ge(h_high, (c + 1) * KT + k - 3)
                                turn_x(c + 1, k, k % 4)
                        if half == 0:
                            if q == 0:
                                pe.wait_ge(yp_ready, (c + 1) * G)
                                pe.wait_ge(ys_mixed, (c + 1) * G)
                                if first:
                                    pe.wait_ge(gate_ready, 2)
                            pe.wait_ge(yp_low, c * G + q + 1)
                            pe.wait_ge(ys_low, c * G + q + 1)
                        elif q == 0:
                            if last:
                                for _, freed in banks_of_group:
                                    pe.wait_ge(freed, (c + 1) * G)
                            else:
                                pe.wait_ge(h_high, (c + 2) * KT)
                        if last and half:
                            j = q
                            for i in range(4):
                                if j == 0:
                                    pe.wait_ge(w_low, c * UNITS + IN_UNITS + 4 + i + 1)
                                done = token_unit((IN_UNITS + 4 + i) % S_SLOTS, i, (i, G + i), B, yH, yL, (j,))
                            done.then_inc(unit_done, 1)
                        else:
                            token_unit(s, q, (q, G + q), A if half == 0 else B, yH, yL).then_inc(unit_done, 1)

            run_chunks(pe, chunk)
    return nc


def kernel(x, c, w_ada, b_ada, w_in, w_pool, pool_scale, sgu_ln_g, sgu_ln_b, w_sgu, b_sgu, w_out, ln_g, ln_b):
    import numpy as np
    import concourse.bacc as bacc
    from concourse.bass_utils import run_bass_kernel_spmd

    x, c, w_ada, b_ada, w_in, w_out = (np.asarray(a) for a in (x, c, w_ada, b_ada, w_in, w_out))
    d = x.shape[-1]
    kt, half = d // P, d // 2
    wi = w_in[0].reshape(kt, P, w_in.shape[-1])
    wo = w_out[0].reshape(kt, P, d)
    col_xa, col_ga, col_u, col_v, col_gb = 0, half, 2 * half, 3 * half, 4 * half

    def by_rows(blocks):
        return np.ascontiguousarray(np.transpose(blocks, (1, 0, 2))).reshape(P, -1)

    units = [by_rows(wi[2 * q:2 * q + 2, :, col_v:col_v + T]) for q in range(V_UNITS)]
    for g in range(G):
        units += [by_rows(wi[:, :, col + g * P:col + (g + 1) * P]) for col in (col_xa, col_ga, col_u, col_gb)]
    for h in range(2):
        units += [by_rows(wo[q::G, :, h * half:(h + 1) * half]) for q in range(G)]
    wa = w_ada[0].reshape(kt, P, 3, d)
    mods = []
    for q in range(4):
        pair = wa[:, :, 0:2, 2 * q * P:2 * (q + 1) * P].reshape(kt, P, T)
        mods += [by_rows(pair[2 * r:2 * r + 2]) for r in range(4)]
    mods += [wa[k, :, 2] for k in range(kt)]
    vectors = np.concatenate([c.reshape(-1, P), b_ada[0, :2 * d].reshape(-1, P),
                              np.asarray(pool_scale)[0].reshape(-1, P), np.asarray(sgu_ln_g)[0].reshape(-1, P)])
    arrays = {
        "x": x[0],
        "w_units": np.stack(units),
        "mod_units": np.stack(mods),
        "vectors": vectors,
        "b_gate": b_ada[:, 2 * d:],
        "ln_g": np.asarray(ln_g),
        "ln_b": np.asarray(ln_b),
        "sgu_b": np.asarray(sgu_ln_b).reshape(1, -1),
        "b_sgu": np.asarray(b_sgu).reshape(1, -1),
        "w_pool": np.asarray(w_pool)[0],
        "w_sgu": np.asarray(w_sgu)[0],
    }
    arrays = {name: np.ascontiguousarray(a) for name, a in arrays.items()}
    nc = bacc.Bacc("TRN2", target_bir_lowering=False, num_devices=1)
    handles = [nc.dram_tensor("in_" + name, a.shape, mybir.dt.from_np(a.dtype), kind="ExternalInput").ap()
               for name, a in arrays.items()]
    out = nc.dram_tensor("out", x[0].shape, F32, kind="ExternalOutput").ap()
    hybrid_layer(nc, *handles, out)
    result = run_bass_kernel_spmd(nc, [{"in_" + name: a for name, a in arrays.items()}], core_ids=[0])
    return result.results[0]["out"].reshape(x.shape)
```

```python
from contextlib import ExitStack

import concourse.bass as bass
from concourse import mybir

ALU = mybir.AluOpType
ACT = mybir.ActivationFunctionType
F32 = mybir.dt.float32
F32R = mybir.dt.float32r

P = 128
T = 512
TILES = T // P
G = 4
WINDOWS = (2, 4, 8, 16)
HALO = 16
EPS = 1e-5

V_UNITS = 4
IN_UNITS = V_UNITS + 4 * G
OUT_UNITS = 8
UNITS = IN_UNITS + OUT_UNITS
F_SLOTS = 2
S_SLOTS = 4
AHEAD = 2
MOD_COLS = 16
MOD_UNITS = 24
POOL_AFTER = (7, 10, 14, 18)
SGU_AFTER = (8, 10, 14, 18)
X_STATS_IN = {10: 0, 11: 1, 14: 2, 15: 3}
X_NORM_IN = {11: 0, 14: 1, 15: 2, 18: 3}
GATE_LOADS_IN = {5: 16, 6: 17, 7: 18, 8: 19, 9: 20, 10: 21, 11: 22, 12: 23}
GATE_BEFORE_RSTD = (4, 5, 8, 8)
GATE_SCALE_FROM = 8
M_SLOTS = 6
GATE_SLOTS = 4
PE_MODS = (0, 1)
DVE_MODS = tuple(m for m in range(MOD_COLS) if m not in PE_MODS)
GATE_UNITS = MOD_UNITS - MOD_COLS
MODC_AT = 0
HSPLIT_AT = 5
MOD_TILE = 1
WARM = (18, 0, 1, 0, 5)
V_C, V_SHIFT, V_SCALE, V_PS, V_LG, V_ROWS = 0, 8, 16, 24, 28, 32


class Steps:

    def __init__(self, sem, per_chunk):
        self.sem, self.per_chunk, self.n = sem, per_chunk, per_chunk

    def begin(self, chunk):
        assert self.n == self.per_chunk
        self.chunk, self.n = chunk, 0

    def then(self, eng, instruction):
        self.n += 1
        instruction.then_inc(self.sem, 1)
        eng.wait_ge(self.sem, self.chunk * self.per_chunk + self.n)


def hybrid_layer(nc, x, w_units, mod_units, vectors, b_gate, ln_g, ln_b, sgu_b, b_sgu, w_pool, w_sgu, out):
    D = x.shape[1]
    KT = D // P
    HALF = D // 2
    CHUNKS = x.shape[0] // T
    ALPHA = 2.0 ** 0.25
    assert D == 1024 and KT == 8 and CHUNKS >= 3 and UNITS % S_SLOTS == 0

    x_tiles = x.rearrange("(c j p) d -> c j p d", j=TILES, p=P)
    out_tiles = out.rearrange("(c j p) d -> c j p d", j=TILES, p=P)

    with ExitStack() as ctx:
        def sb(name, shape, dt=F32):
            return ctx.enter_context(nc.sbuf_tensor(name, shape, dt))

        def sem(name):
            return ctx.enter_context(nc.semaphore(name))

        hH, hL = sb("h_high", [P, KT, T], F32R), sb("h_low", [P, KT, T], F32R)
        yH, yL = sb("y_high", [P, KT, T], F32R), sb("y_low", [P, KT, T], F32R)
        wF = sb("w_float", [P, F_SLOTS, 1024])
        wH, wL = sb("w_high", [P, S_SLOTS, 1024], F32R), sb("w_low", [P, S_SLOTS, 1024], F32R)
        xn = sb("x_norm", [P, TILES, D])
        z = sb("z", [P, TILES, D])
        lngB, lnbB, gateB = sb("ln_g_rows", [P, D]), sb("ln_b_rows", [P, D]), sb("gate_rows", [P, D])
        gv = sb("v_gelu", [P, TILES, T])
        vH, vL = sb("v_high", [P, TILES, T], F32R), sb("v_low", [P, TILES, T], F32R)
        wt = sb("w_sgu_parts", [P, G, 2, P], F32R)
        wpH, wpL = sb("w_pool_high", [P, G, P], F32R), sb("w_pool_low", [P, G, P], F32R)
        E = sb("sgu_bias", [P, G, P])
        ident, ones = sb("identity", [P, P]), sb("ones", [P, P])
        X = sb("xa", [P, HALO + T])
        S = [sb("sum_a", [P, HALO + T]), sb("sum_b", [P, HALO + T])]
        hF = [s[:, HALO:] for s in S]
        halo = sb("xa_halo", [P, G, HALO])
        pH, pL = sb("pooled_high", [P, T], F32R), sb("pooled_low", [P, T], F32R)
        tanh = sb("tanh", [P, T])
        sga, sgb = sb("gate_a", [P, T]), sb("gate_b", [P, T])
        ug = sb("u_gelu", [P, T])
        mixed = sb("mixed", [P, T])
        yP = sb("y_pool", [P, T])
        vec_rows = sb("vector_rows", [V_ROWS, P])
        cols = sb("vector_cols", [P, V_ROWS])
        ctanh = sb("c_tanh", [P, KT])
        csilu = sb("c_silu", [P, KT])
        modc = sb("mod_cols", [P, KT // 2, 4])
        halfc = sb("half_cols", [P, 2 * G])
        count_inv = sb("count_inv", [P, HALO])
        minus_half = sb("minus_half", [P, G])
        xst, xmv = sb("x_stats", [P, TILES, 2, 6]), sb("x_mean_var", [P, TILES, 2])
        zst, zmv = sb("z_stats", [P, TILES, 2, 6]), sb("z_mean_var", [P, TILES, 2])
        vst, vmv = sb("v_stats", [P, TILES, G, 6]), sb("v_mean_var", [P, TILES, G, 2])
        xve, xrs = sb("x_var_eps", [P, TILES]), sb("x_rstd", [P, TILES])
        xoff, zoff = sb("x_offset", [P, TILES]), sb("z_offset", [P, TILES])
        zve, zrs = sb("z_var_eps", [P, TILES]), sb("z_rstd", [P, TILES])
        vve, vrs = sb("v_var_eps", [P, TILES, G]), sb("v_rstd", [P, TILES, G])
        spare = sb("spare", [P, 1])
        macc = gv
        wtF, wpF, sgubB, wsN = gateB[:, 0:HALF], sgb, mixed, yP
        bsgu_row, bgate_row = ug[0:1, :], z[0:1, 0, :]

        A = ctx.enter_context(nc.psum_tensor("bank_a", [P, 4, T], F32))
        B = ctx.enter_context(nc.psum_tensor("bank_b", [P, 4, T], F32))

        w_landed = [sem(f"w_landed{i}") for i in range(F_SLOTS)]
        m_landed = [sem(f"m_landed{i}") for i in range(M_SLOTS)]
        xn_landed = [sem(f"xn_landed{j}") for j in range(TILES)]
        z_landed = [sem(f"z_landed{j}") for j in range(TILES)]
        z_stored = [sem(f"z_stored{j}") for j in range(TILES)]
        vec_landed, small_landed, rows_landed = sem("vec_landed"), sem("small_landed"), sem("rows_landed")
        wsgu_landed, bgate_landed = sem("wsgu_landed"), sem("b_gate_landed")
        const_ready, ident_zero, mask_ready = sem("const_ready"), sem("ident_zero"), sem("mask_ready")
        x_rstd, v_rstd, z_rstd = sem("x_rstd_ready"), sem("v_rstd_ready"), sem("z_rstd_ready")
        w_high, w_low = sem("w_high_ready"), sem("w_low_ready")
        unit_done = sem("unit_done")
        vec_turned, vec_ready, c_tanh, c_ready = sem("vec_turned"), sem("vec_ready"), sem("c_tanh_ready"), sem("c_ready")
        mod_multiplied, mod_used = sem("mod_unit_used_by_tensor"), sem("mod_unit_used_by_vector")
        gate_scaled, gate_added = sem("gate_unit_scaled"), sem("gate_unit_added")
        mod_summed, mod_ready = sem("mod_summed"), sem("mod_ready")
        wt_turned, wt_ready, e_done = sem("wt_turned"), sem("wt_ready"), sem("e_done")
        small_high, small_low = sem("small_high"), sem("small_low")
        gate_summed, gate_ready = sem("gate_summed"), sem("gate_ready")
        setup = Steps(sem("setup_steps"), 0)
        x_offset = sem("x_offset_ready")
        x_stats, x_ready, x_turned = sem("x_stats_ready"), sem("x_norm_ready"), sem("x_turned")
        h_float, h_high, h_low = sem("h_float_ready"), sem("h_high_ready"), sem("h_low_ready")
        v_gelu, v_stats, v_norm = sem("v_gelu_ready"), sem("v_stats_ready"), sem("v_norm_ready")
        v_high, v_low = sem("v_high_ready"), sem("v_low_ready")
        xa_copied, pooled, p_high, p_low = sem("xa_copied"), sem("pooled_ready"), sem("p_high_ready"), sem("p_low_ready")
        ga_tanh, ga_gated, gb_tanh, gb_gated = sem("ga_tanh"), sem("ga_gated"), sem("gb_tanh"), sem("gb_gated")
        u_gelu = sem("u_gelu_ready")
        pool_done, sgu_done = sem("pool_product_done"), sem("sgu_product_done")
        yp_ready, yp_high, yp_low = sem("yp_ready"), sem("yp_high_ready"), sem("yp_low_ready")
        ys_mixed, ys_ready, ys_high, ys_low = sem("sgu_mixed"), sem("ys_ready"), sem("ys_high_ready"), sem("ys_low_ready")
        z_added, z_stats, z_ready = sem("z_added"), sem("z_stats_ready"), sem("z_ready")
        tail_offset, tail_normed, tail_scaled = sem("tail_offset"), sem("tail_normed"), sem("tail_scaled")
        tail_added, tail_halves = sem("tail_added"), sem("tail_half_ready")
        pool_steps = Steps(sem("pool_steps"), sum(range(2, 2 + G)) + 2 * G)
        v_steps, x_steps = Steps(sem("v_steps"), 2 * TILES), Steps(sem("x_steps"), 2 * TILES)
        z_steps = [Steps(sem("z_first_half_steps"), TILES), Steps(sem("z_second_half_steps"), 4 * TILES)]

        def wait(eng, s, value):
            if not isinstance(value, int) or value > 0:
                eng.wait_ge(s, value)

        def run_chunks(eng, chunk):
            chunk(0, True, False)
            with eng.Fori(1, CHUNKS - 1) as c:
                chunk(c, False, False)
            chunk(CHUNKS - 1, False, True)

        def m_sem(m):
            return m % M_SLOTS if m < MOD_COLS else m % GATE_SLOTS

        def m_slot(m):
            n = m_sem(m)
            return z[:, n, :] if n < TILES else (lngB, lnbB)[n - TILES][:, :]

        def m_wait(eng, m):
            nth = sum(1 for i in range(m + 1) if m_sem(i) == m_sem(m))
            eng.wait_ge(m_landed[m_sem(m)], nth * 16)

        block = ctx.enter_context(nc.Block())

        @block.sync
        def _(sp):
            def load_w(c, n):
                wait(sp, w_low, c * UNITS + n - F_SLOTS + 1)
                sp.dma_start(wF[:, n % F_SLOTS, :], w_units[n % UNITS]).then_inc(w_landed[n % F_SLOTS], 16)

            def load_m(m):
                before = m - M_SLOTS
                if m == MOD_COLS:
                    before = MOD_COLS - 1
                elif m > MOD_COLS:
                    before = m - GATE_SLOTS
                if before in PE_MODS:
                    sp.wait_ge(mod_multiplied, PE_MODS.index(before) + 1)
                elif before >= MOD_COLS:
                    if before == MOD_COLS:
                        sp.wait_ge(gate_scaled, 1)
                    else:
                        sp.wait_ge(gate_added, before - MOD_COLS)
                elif before > 0:
                    sp.wait_ge(mod_used, DVE_MODS.index(before) + 1)
                sp.dma_start(m_slot(m), mod_units[m]).then_inc(m_landed[m_sem(m)], 16)

            sp.dma_start(vec_rows[:, :], vectors).then_inc(vec_landed, 16)
            for j in range(TILES):
                sp.dma_start(xn[:, j, :], x_tiles[0, j]).then_inc(xn_landed[j], 16)
                if j in (1, 2):
                    load_m(j - 1)
            for q in range(V_UNITS):
                for m in range(max(4 * q, 2), 4 * q + 4):
                    load_m(m)
                load_w(0, q)
                if q == V_UNITS - 1:
                    sp.dma_start(wsN[:, :].rearrange("p (h s) -> p h s", h=G),
                                 w_sgu.rearrange("h t s -> t h s")).then_inc(wsgu_landed, 16)
                    sp.dma_start(wpF[:, :].rearrange("p (g d) -> p g d", g=G),
                                 w_pool.rearrange("g c d -> c g d")).then_inc(small_landed, 16)
                    sp.dma_start(sgubB[:, :], sgu_b.broadcast_to([P, G * P])).then_inc(small_landed, 16)
                    sp.dma_start(bsgu_row, b_sgu).then_inc(small_landed, 16)

            def chunk(c, first, last):
                for n in range(UNITS):
                    if n + 2 * AHEAD < UNITS or not last:
                        load_w(c, n + 2 * AHEAD)
                    if first and n == 7:
                        sp.dma_start(lngB[:, :], ln_g.broadcast_to([P, D])).then_inc(rows_landed, 16)
                        sp.dma_start(lnbB[:, :], ln_b.broadcast_to([P, D])).then_inc(rows_landed, 16)
                    if first and n in GATE_LOADS_IN:
                        load_m(GATE_LOADS_IN[n])
                    if first and n == 16:
                        sp.wait_ge(gate_added, GATE_UNITS - GATE_SLOTS)
                        sp.dma_start(bgate_row, b_gate).then_inc(bgate_landed, 16)
                    if not first and 2 <= n < 2 + TILES:
                        j = n - 2
                        sp.wait_ge(z_ready, (c - 1) * TILES + j + 1)
                        sp.dma_start(out_tiles[c - 1, j], z[:, j, :]).then_inc(z_stored[j], 16)
                    if not last and 6 <= n < 6 + TILES:
                        j = n - 6
                        sp.wait_ge(x_turned, (c + 1) * KT)
                        sp.dma_start(xn[:, j, :], x_tiles[c + 1, j]).then_inc(xn_landed[j], 16)
                    if 17 <= n < 17 + TILES:
                        j = n - 17
                        if first:
                            sp.wait_ge(gate_added, GATE_UNITS - 1)
                            sp.wait_ge(gate_summed, 2)
                        else:
                            sp.wait_ge(z_stored[j], c * 16)
                        sp.dma_start(z[:, j, :], x_tiles[c, j]).then_inc(z_landed[j], 16)

            run_chunks(sp, chunk)
            for j in range(2):
                sp.wait_ge(z_ready, (CHUNKS - 1) * TILES + j + 1)
                sp.dma_start(out_tiles[CHUNKS - 1, j], z[:, j, :]).then_inc(z_stored[j], 16)
            for half in range(2):
                if half:
                    sp.wait_ge(tail_added, 2)
                    sp.dma_start(out_tiles[CHUNKS - 1, 2], z[:, 2, :]).then_inc(z_stored[2], 16)
                cut = slice(half * HALF, (half + 1) * HALF)
                sp.wait_ge(tail_halves, half + 1)
                sp.dma_start(out_tiles[CHUNKS - 1, 3][:, cut], z[:, 3, cut]).then_inc(z_stored[3], 16)
            for j in range(TILES):
                sp.wait_ge(z_stored[j], (CHUNKS + (j == 3)) * 16)

        @block.gpsimd
        def _(pool):
            nc.gpsimd.memset(ident[:, :], 0.0).then_inc(ident_zero, 1)
            nc.gpsimd.memset(ones[:, :], 1.0).then_inc(const_ready, 1)
            nc.gpsimd.memset(minus_half[:, :], -0.5).then_inc(const_ready, 1)
            nc.gpsimd.memset(halo[:, :, :], 0.0).then_inc(const_ready, 1)
            pool.wait_ge(ident_zero, 1)
            nc.gpsimd.affine_select(out=ident[:, :], in_=ident[:, :], compare_op=ALU.not_equal, fill=1.0, base=0,
                                    pattern=[[-1, P]], channel_multiplier=1).then_inc(const_ready, 1)

            def rstd(ready, var_eps, rstd_out, exponent):
                nc.gpsimd.tensor_tensor(rstd_out, var_eps, exponent, ALU.pow).then_inc(ready, 1)

            def x_rstds(c, j):
                pool.wait_ge(x_stats, c * TILES + j + 1)
                rstd(x_rstd, xve[:, j:j + 1], xrs[:, j:j + 1], minus_half[:, 0:1])

            pool.wait_ge(const_ready, 4)
            for j in range(TILES):
                x_rstds(0, j)
            for t in range(HALO):
                nc.gpsimd.memset(count_inv[:, t:t + 1], 1.0 / (t + 1)).then_inc(const_ready, 1)
            for n in range(V_UNITS):
                pool.wait_ge(w_high, n + 1)
                nc.gpsimd.tensor_tensor(wL[:, n, :], wF[:, n % F_SLOTS, :], wH[:, n, :].bitcast(F32), ALU.subtract)\
                    .then_inc(w_low, 1)
                if 0 < n < V_UNITS - 1:
                    for k in (2 * n, 2 * n + 1):
                        pool.wait_ge(h_low, k)
                        pool.wait_ge(h_high, k + 1)
                        nc.gpsimd.tensor_tensor(hL[:, k, :], hF[k % 2], hH[:, k, :].bitcast(F32), ALU.subtract)\
                            .then_inc(h_low, 1)
            pool.wait_ge(wsgu_landed, 16)
            ws = wsN[:, :].rearrange("p (h s) -> p h s", h=G)
            nc.gpsimd.affine_select(out=ws, in_=ws, compare_op=ALU.is_ge, fill=0.0, base=0,
                                    pattern=[[0, G], [-1, P]], channel_multiplier=1).then_inc(mask_ready, 1)

            def z_rstds(c, j):
                pool.wait_ge(z_stats, c * TILES + j + 1)
                rstd(z_rstd, zve[:, j:j + 1], zrs[:, j:j + 1], minus_half[:, 0:1])

            def gate_sum(k):
                pool.wait_ge(gate_scaled, k + 1)
                if k > 1:
                    pool.wait_ge(gate_added, k - 1)
                nc.gpsimd.tensor_tensor(gateB[:, :], gateB[:, :], m_slot(MOD_COLS + k), ALU.add)\
                    .then_inc(gate_added, 1)

            def chunk(c, first, last):
                if not first:
                    for j in range(TILES):
                        z_rstds(c - 1, j)
                for j in range(TILES):
                    pool.wait_ge(v_stats, c * TILES + j + 1)
                    rstd(v_rstd, vve[:, j, :], vrs[:, j, :], minus_half[:, :])
                if not last:
                    for j in range(TILES):
                        if first:
                            for k in range(GATE_BEFORE_RSTD[j - 1] if j else 1, GATE_BEFORE_RSTD[j]):
                                gate_sum(k)
                        x_rstds(c + 1, j)

            run_chunks(pool, chunk)

            def tail_offset_of(j):
                pool.wait_ge(z_rstd, (CHUNKS - 1) * TILES + j + 1)
                nc.gpsimd.tensor_scalar(zoff[:, j:j + 1], zmv[:, j, 0:1], zrs[:, j:j + 1], -1.0,
                                        ALU.mult, ALU.mult).then_inc(tail_offset, 1)

            def tail_scale(j, cut):
                pool.wait_ge(tail_normed, j)
                nc.gpsimd.tensor_tensor(z[:, j, cut], z[:, j, cut], lngB[:, cut], ALU.mult).then_inc(tail_scaled, 1)

            z_rstds(CHUNKS - 1, 0)
            z_rstds(CHUNKS - 1, 1)
            tail_offset_of(1)
            tail_scale(1, slice(0, D))
            z_rstds(CHUNKS - 1, 2)
            tail_offset_of(2)
            tail_scale(2, slice(0, HALF))
            z_rstds(CHUNKS - 1, 3)
            for half in range(2):
                cut = slice(half * HALF, (half + 1) * HALF)
                pool.wait_ge(tail_scaled, half + 2)
                nc.gpsimd.tensor_tensor(z[:, 2, cut], z[:, 2, cut], lnbB[:, cut], ALU.add).then_inc(tail_added, 1)

        @block.scalar
        def _(act):
            def split_high(c, n):
                wait(act, unit_done, c * UNITS + n - S_SLOTS + 1)
                act.wait_ge(w_landed[n % F_SLOTS], (c * (UNITS // F_SLOTS) + n // F_SLOTS + 1) * 16)
                nc.scalar.activation(wH[:, n % S_SLOTS, :], wF[:, n % F_SLOTS, :], ACT.Copy).then_inc(w_high, 1)

            def h_evacuate(c, k):
                act.wait_ge(x_turned, c * KT + k + 1)
                wait(act, h_low, c * KT + k - 1)
                bank = B[:, k % 3 if isinstance(c, int) and c == 0 else k % 4, :]
                shift, scale = modc[:, k // 2, k % 2:k % 2 + 1], modc[:, k // 2, 2 + k % 2:3 + k % 2]
                nc.scalar.activation(hF[k % 2], bank, ACT.Identity, bias=shift, scale=scale).then_inc(h_float, 1)
                nc.scalar.activation(hH[:, k, :], bank, ACT.Identity, bias=shift, scale=scale).then_inc(h_high, 1)

            act.wait_ge(vec_turned, 1)
            nc.scalar.activation(cols[:, :], B[:, 3, 0:V_ROWS], ACT.Copy).then_inc(vec_ready, 1)
            act.wait_ge(vec_ready, 1)
            nc.scalar.activation(ctanh[:, :], cols[:, V_C:V_C + KT], ACT.Tanh, scale=0.5).then_inc(c_tanh, 1)
            for j in range(TILES):
                act.wait_ge(x_offset, j + 1)
                nc.scalar.activation(xn[:, j, :], xn[:, j, :], ACT.Identity, bias=xoff[:, j:j + 1],
                                     scale=xrs[:, j:j + 1]).then_inc(x_ready, 1)
            for q in range(V_UNITS):
                split_high(0, q)
                act.wait_ge(mod_ready, q + 1)
                h_evacuate(0, 2 * q)
                h_evacuate(0, 2 * q + 1)
            def small_weights():
                act.wait_ge(wt_turned, 1)
                nc.scalar.activation(wtF, B[:, 3, :], ACT.Copy).then_inc(wt_ready, 1)
                nc.scalar.activation(wt[:, :, 0, :], B[:, 3, :].rearrange("p (h t) -> p h t", h=G), ACT.Copy)\
                    .then_inc(small_high, 1)
                act.wait_ge(small_landed, 48)
                nc.scalar.activation(wpH[:, :, :].rearrange("p g d -> p (g d)"), wpF[:, :], ACT.Copy)\
                    .then_inc(small_high, 1)

            def sgu_bias():
                act.wait_ge(e_done, 1)
                nc.scalar.activation(E[:, :, :].rearrange("p h t -> p (h t)"), B[:, 3, :], ACT.Copy, scale=0.5)\
                    .then_inc(small_high, 1)

            def chunk(c, first, last):
                for n in range(UNITS):
                    if (n + AHEAD < UNITS or not last) and not (first and n + AHEAD < V_UNITS):
                        split_high(c, n + AHEAD)
                    if n == V_UNITS:
                        act.wait_ge(unit_done, c * UNITS + V_UNITS)
                        for j in range(TILES):
                            nc.scalar.activation(gv[:, j, :], A[:, j, :], ACT.Gelu).then_inc(v_gelu, 1)
                    g, step = (n - V_UNITS - 1) // 4, (n - V_UNITS - 1) % 4
                    if n > V_UNITS and g < G:
                        act.wait_ge(unit_done, c * UNITS + n)
                        if step == 0:
                            wait(act, pooled, c * G + g)
                            nc.scalar.activation(X[:, HALO:], B[:, 0, :], ACT.Copy).then_inc(xa_copied, 1)
                        if step == 1:
                            nc.scalar.activation(tanh[:, :], B[:, 1, :], ACT.Tanh, scale=0.5).then_inc(ga_tanh, 1)
                            act.wait_ge(pooled, c * G + g + 1)
                            nc.scalar.activation(pH[:, :], S[(g + 1) % 2][:, HALO:], ACT.Copy).then_inc(p_high, 1)
                        if step == 2:
                            wait(act, ys_mixed, c * G + g)
                            nc.scalar.activation(ug[:, :], B[:, 2, :], ACT.Gelu).then_inc(u_gelu, 1)
                        if step == 3:
                            act.wait_ge(ga_gated, c * G + g + 1)
                            nc.scalar.activation(tanh[:, :], B[:, 3, :], ACT.Tanh, scale=0.5).then_inc(gb_tanh, 1)
                    for g in range(G):
                        if n == POOL_AFTER[g] + 2:
                            act.wait_ge(yp_ready, c * G + g + 1)
                            nc.scalar.activation(yH[:, g, :], yP[:, :], ACT.Copy).then_inc(yp_high, 1)
                        if n == SGU_AFTER[g] + 2:
                            act.wait_ge(ys_ready, c * G + g + 1)
                            nc.scalar.activation(yH[:, G + g, :], mixed[:, :], ACT.Copy).then_inc(ys_high, 1)
                    if first and n == V_UNITS + 1:
                        small_weights()
                    if first and n == V_UNITS + 2:
                        sgu_bias()
                    if V_UNITS < n <= V_UNITS + 2:
                        for j in range(2 * (n - V_UNITS - 1), 2 * (n - V_UNITS)):
                            act.wait_ge(v_norm, c * TILES + j + 1)
                            nc.scalar.activation(vH[:, j, :], gv[:, j, :], ACT.Copy).then_inc(v_high, 1)
                    if first and GATE_SCALE_FROM <= n < GATE_SCALE_FROM + GATE_UNITS:
                        k = n - GATE_SCALE_FROM
                        m_wait(act, MOD_COLS + k)
                        if k == 0:
                            act.wait_ge(c_ready, 3)
                            act.wait_ge(small_low, 1)
                            act.wait_ge(e_done, 1)
                        rows = m_slot(MOD_COLS + k)
                        nc.scalar.activation(rows if k else gateB[:, :], rows, ACT.Copy, scale=csilu[:, k:k + 1])\
                            .then_inc(gate_scaled, 1)
                    if first and n == IN_UNITS - 1:
                        act.wait_ge(gate_summed, 2)
                        for half, bank in enumerate((A[:, 0, :], B[:, 0, :])):
                            nc.scalar.activation(gateB[:, half * HALF:(half + 1) * HALF], bank, ACT.Copy)\
                                .then_inc(gate_ready, 1)
                    if not last and IN_UNITS <= n < IN_UNITS + 4:
                        for k in range(2 * (n - IN_UNITS), 2 * (n - IN_UNITS) + 2):
                            h_evacuate(c + 1, k)

            run_chunks(act, chunk)
            for j in (1, 2):
                act.wait_ge(tail_offset, j)
                nc.scalar.activation(z[:, j, :], z[:, j, :], ACT.Identity, bias=zoff[:, j:j + 1],
                                     scale=zrs[:, j:j + 1]).then_inc(tail_normed, 1)

        @block.vector
        def _(dve):
            vec = nc.vector

            def split_low(c, n):
                dve.wait_ge(w_high, c * UNITS + n + 1)
                vec.tensor_tensor(wL[:, n % S_SLOTS, :], wF[:, n % F_SLOTS, :],
                                  wH[:, n % S_SLOTS, :].bitcast(F32), ALU.subtract).then_inc(w_low, 1)

            def h_split(c, k):
                dve.wait_ge(h_high, c * KT + k + 1)
                vec.tensor_tensor(hL[:, k, :], hF[k % 2], hH[:, k, :].bitcast(F32), ALU.subtract).then_inc(h_low, 1)

            def aggregate(steps, out_stats, in_stats, last_stats):
                steps.then(dve, last_stats)
                vec.memset(spare[:, :], 0.0)
                for o, i in zip(out_stats, in_stats):
                    last = vec.bn_aggr(o, i)
                steps.then(dve, last)

            def x_stats_of(c, j):
                dve.wait_ge(xn_landed[j], (c + 1) * 16)
                for h in range(2):
                    last = vec.bn_stats(xst[:, j, h, :], xn[:, j, h * HALF:(h + 1) * HALF])
                aggregate(x_steps, [xmv[:, j, :]], [xst[:, j, :, :].rearrange("p a b -> p (a b)")], last)
                vec.tensor_scalar(xve[:, j:j + 1], xmv[:, j, 1:2], EPS, None, ALU.add).then_inc(x_stats, 1)

            def x_norm_of(c, j):
                dve.wait_ge(x_rstd, c * TILES + j + 1)
                vec.tensor_scalar(xn[:, j, :], xn[:, j, :], xmv[:, j, 0:1], xrs[:, j:j + 1],
                                  ALU.subtract, ALU.mult).then_inc(x_ready, 1)

            def mod_sum(m, between=None):
                m_wait(dve, m)
                acc = macc[:, m // 4, :]
                for a in range(2):
                    rows, c_col = m_slot(m)[:, a * T:(a + 1) * T], csilu[:, 2 * (m % 4) + a:2 * (m % 4) + a + 1]
                    if (m % 4 == 0 or m - 1 in PE_MODS) and a == 0:
                        ins = vec.tensor_scalar(acc, rows, c_col, None, ALU.mult)
                    else:
                        ins = vec.scalar_tensor_tensor(out=acc, in0=rows, scalar=c_col, in1=acc,
                                                       op0=ALU.mult, op1=ALU.add)
                    if a == 0:
                        setup.then(dve, ins)
                        if between:
                            between()
                ins.then_inc(mod_used, 1)
                dve.wait_ge(mod_used, DVE_MODS.index(m) + 1)

            setup.begin(0)
            x_steps.begin(0)
            def x_offset_of(j):
                dve.wait_ge(x_rstd, j + 1)
                vec.scalar_tensor_tensor(out=xoff[:, j:j + 1], in0=xmv[:, j, 0:1], scalar=-1.0, in1=xrs[:, j:j + 1],
                                         op0=ALU.mult, op1=ALU.mult).then_inc(x_offset, 1)

            for j in range(TILES):
                x_stats_of(0, j)
                if j == 0:
                    dve.wait_ge(vec_ready, 1)
                    dve.wait_ge(c_tanh, 1)
                    setup.then(dve, vec.scalar_tensor_tensor(out=csilu[:, :], in0=ctanh[:, :], scalar=1.0,
                                                             in1=cols[:, V_C:V_C + KT], op0=ALU.add, op1=ALU.mult))
                    vec.tensor_scalar(csilu[:, :], csilu[:, :], 0.5, None, ALU.mult).then_inc(c_ready, 1)
                    vec.tensor_scalar(halfc[:, :], cols[:, V_PS:V_PS + 2 * G], 0.5, None, ALU.mult).then_inc(c_ready, 1)
                    vec.tensor_scalar(cols[:, V_SCALE:V_SCALE + KT], cols[:, V_SCALE:V_SCALE + KT], 1.0, None,
                                      ALU.add).then_inc(c_ready, 1)
                else:
                    x_offset_of(j - 1)
            dve.wait_ge(c_ready, 3)

            def mod_cols_of(q):
                dve.wait_ge(mod_summed, q + 1)
                bias = cols[:, V_SHIFT:V_SHIFT + 2 * KT].rearrange("p (s k) -> p s k", s=2)[:, :, 2 * q:2 * q + 2]
                vec.tensor_tensor(modc[:, q, :].rearrange("p (s k) -> p s k", s=2),
                                  B[:, 3, 0:4].rearrange("p (s k) -> p s k", s=2), bias, ALU.add).then_inc(mod_ready, 1)

            for m in DVE_MODS:
                if m < MOD_COLS:
                    mod_sum(m, (lambda: mod_cols_of(0)) if m == 4 else None)
                    if m > 4 and m % 4 == MODC_AT:
                        mod_cols_of(m // 4 - 1)
                    if m == DVE_MODS[0]:
                        x_offset_of(TILES - 1)
                    if m == HSPLIT_AT:
                        h_split(0, 0)
                        h_split(0, 1)
            mod_cols_of(V_UNITS - 1)
            for k in (KT - 2, KT - 1):
                dve.wait_ge(h_low, k)
                h_split(0, k)

            dve.wait_ge(w_low, V_UNITS)

            def small_weights():
                dve.wait_ge(small_high, 2)
                vec.tensor_tensor(wt[:, :, 1, :], wtF.rearrange("p (h t) -> p h t", h=G),
                                  wt[:, :, 0, :].bitcast(F32), ALU.subtract)\
                    .then_inc(small_low, 1)
                vec.tensor_tensor(wpL[:, :, :].rearrange("p g d -> p (g d)"), wpF[:, :],
                                  wpH[:, :, :].rearrange("p g d -> p (g d)").bitcast(F32), ALU.subtract)\
                    .then_inc(small_low, 1)

            def pooling(c, g, first):
                w = WINDOWS[g]
                if g == 0 and first:
                    dve.wait_ge(const_ready, 4 + HALO)
                wait(dve, p_low, c * G + g)
                wait(dve, h_low, (c + 1) * KT)
                dve.wait_ge(xa_copied, c * G + g + 1)
                pool_steps.then(dve, vec.tensor_copy(X[:, 0:HALO], halo[:, g, :]))
                src = X
                for level in range(g + 1):
                    shift = 1 << level
                    lo = HALO - (w - 2 * shift)
                    dst = S[level % 2]
                    pool_steps.then(dve, vec.tensor_tensor(dst[:, lo:], src[:, lo:],
                                                           src[:, lo - shift:HALO + T - shift], ALU.add))
                    src = dst
                dst = S[(g + 1) % 2]
                vec.tensor_copy(halo[:, g, :], X[:, T:])
                mean = vec.scalar_tensor_tensor(out=dst[:, HALO:], in0=src[:, HALO:], scalar=1.0 / w,
                                                in1=X[:, HALO:], op0=ALU.mult, op1=ALU.subtract)
                if first:
                    head = slice(HALO, HALO + w - 1)
                    setup.then(dve, mean)
                    setup.then(dve, vec.tensor_tensor(dst[:, head], src[:, head], count_inv[:, 0:w - 1], ALU.mult))
                    mean = vec.tensor_tensor(dst[:, head], dst[:, head], X[:, head], ALU.subtract)
                mean.then_inc(pooled, 1)

            def pooled_low(c, g):
                dve.wait_ge(p_high, c * G + g + 1)
                vec.tensor_tensor(pL[:, :], S[(g + 1) % 2][:, HALO:], pH[:, :].bitcast(F32), ALU.subtract).then_inc(p_low, 1)

            def gate(tanh_ready, gated, out_t, bank, value):
                dve.wait_ge(tanh_ready, value)
                vec.scalar_tensor_tensor(out=out_t[:, :], in0=tanh[:, :], scalar=1.0, in1=B[:, bank, :],
                                         op0=ALU.add, op1=ALU.mult).then_inc(gated, 1)

            def y_pool(c, g):
                dve.wait_ge(pool_done, c * G + g + 1)
                wait(dve, yp_low, c * G + g)
                dve.wait_ge(ga_gated, c * G + g + 1)
                vec.scalar_tensor_tensor(out=yP[:, :], in0=A[:, g % 2, :], scalar=halfc[:, g:g + 1], in1=sga[:, :],
                                         op0=ALU.mult, op1=ALU.mult).then_inc(yp_ready, 1)

            def mix(c, g, first):
                dve.wait_ge(sgu_done, c * G + g + 1)
                wait(dve, ys_low, c * G + g)
                if first and g == 0:
                    dve.wait_ge(small_high, 3)
                scale = halfc[:, G + g:G + g + 1]
                summed = mixed[:, :].rearrange("p (j t) -> p j t", j=TILES)
                parts = A[:, 2:4, :].rearrange("p b (j r t) -> p (b j) r t", j=TILES // 2, r=2)
                addend = E[:, g:g + 1, :].broadcast_to([P, TILES, P])
                for part in range(2):
                    pool_steps.then(dve, vec.scalar_tensor_tensor(out=summed, in0=parts[:, :, part, :], scalar=scale,
                                                                  in1=addend, op0=ALU.mult, op1=ALU.add))
                    addend = summed
                dve.wait_ge(u_gelu, c * G + g + 1)
                vec.tensor_tensor(mixed[:, :], mixed[:, :], ug[:, :], ALU.mult).then_inc(ys_mixed, 1)

            def y_low(c, g, high, low, row, src):
                dve.wait_ge(high, c * G + g + 1)
                vec.tensor_tensor(yL[:, row, :], src[:, :], yH[:, row, :].bitcast(F32), ALU.subtract).then_inc(low, 1)

            def v_stats_of(c, j):
                dve.wait_ge(v_gelu, c * TILES + j + 1)
                for h in range(G):
                    last = vec.bn_stats(vst[:, j, h, :], gv[:, j, h * P:(h + 1) * P])
                aggregate(v_steps, [vmv[:, j, h, :] for h in range(G)], [vst[:, j, h, :] for h in range(G)], last)
                vec.tensor_scalar(vve[:, j, :], vmv[:, j, :, 1], EPS, None, ALU.add).then_inc(v_stats, 1)

            def v_norm_of(c, j):
                dve.wait_ge(v_rstd, c * TILES + j + 1)
                for h in range(G):
                    head = gv[:, j, h * P:(h + 1) * P]
                    last = vec.tensor_scalar(head, head, vmv[:, j, h, 0:1], vrs[:, j, h:h + 1], ALU.subtract, ALU.mult)
                last.then_inc(v_norm, 1)

            def v_low_of(c, j):
                dve.wait_ge(v_high, c * TILES + j + 1)
                vec.tensor_tensor(vL[:, j, :], gv[:, j, :], vH[:, j, :].bitcast(F32), ALU.subtract).then_inc(v_low, 1)

            def z_half(c, j, half, bank):
                cut = slice(half * HALF, (half + 1) * HALF)
                if half == 0:
                    dve.wait_ge(z_landed[j], (c + 1) * 16)
                product = vec.tensor_tensor(tanh[:, :], bank[:, j, :], gateB[:, cut], ALU.mult)
                product.then_inc(z_added, 1)
                dve.wait_ge(z_added, c * 2 * TILES + half * TILES + j + 1)
                z_steps[half].then(dve, vec.scalar_tensor_tensor(out=z[:, j, cut], in0=z[:, j, cut], scalar=ALPHA,
                                                                 in1=tanh[:, :], op0=ALU.mult, op1=ALU.add))
                stats = vec.bn_stats(zst[:, j, half, :], z[:, j, cut])
                if half:
                    aggregate(z_steps[1], [zmv[:, j, :]], [zst[:, j, :, :].rearrange("p a b -> p (a b)")], stats)
                    vec.tensor_scalar(zve[:, j:j + 1], zmv[:, j, 1:2], EPS, None, ALU.add).then_inc(z_stats, 1)

            def z_norm(c, j):
                dve.wait_ge(z_rstd, c * TILES + j + 1)
                z_steps[1].then(dve, vec.scalar_tensor_tensor(out=z[:, j, :], in0=z[:, j, :], scalar=zmv[:, j, 0:1],
                                                              in1=lngB[:, :], op0=ALU.subtract, op1=ALU.mult))
                vec.scalar_tensor_tensor(out=z[:, j, :], in0=z[:, j, :], scalar=zrs[:, j:j + 1], in1=lnbB[:, :],
                                         op0=ALU.mult, op1=ALU.add).then_inc(z_ready, 1)

            def chunk(c, first, last):
                for steps in (pool_steps, v_steps, z_steps[0]):
                    steps.begin(c)
                if not first:
                    z_steps[1].begin(c - 1)
                if not last:
                    x_steps.begin(c + 1)
                for n in range(UNITS):
                    if (n + AHEAD < UNITS or not last) and not (first and n + AHEAD < V_UNITS):
                        split_low(c, n + AHEAD)
                    if not first and n < TILES + 1:
                        if n < TILES:
                            if n == 0:
                                dve.wait_ge(unit_done, c * UNITS)
                            z_half(c - 1, n, 1, B)
                        if n > 0:
                            z_norm(c - 1, n - 1)
                    if n == V_UNITS:
                        v_stats_of(c, 0)
                        v_stats_of(c, 1)
                        v_norm_of(c, 0)
                    g, step = (n - V_UNITS - 1) // 4, (n - V_UNITS - 1) % 4
                    if n > V_UNITS and g < G:
                        if step == 0:
                            pooling(c, g, first)
                        if step == 1:
                            pooled_low(c, g)
                            gate(ga_tanh, ga_gated, sga, 1, c * G + g + 1)
                        if step == 3:
                            if first and g == 0:
                                dve.wait_ge(small_low, 2)
                            gate(gb_tanh, gb_gated, sgb, 3, c * G + g + 1)
                    if first and n == V_UNITS + 2:
                        small_weights()
                    for g in range(G):
                        if n == POOL_AFTER[g] + 1:
                            y_pool(c, g)
                        if n == SGU_AFTER[g] + 1:
                            mix(c, g, first)
                        if n == SGU_AFTER[g] + 2:
                            dve.wait_ge(ys_mixed, c * G + g + 1)
                            dve.wait_ge(gb_gated, c * G + g + 1)
                            vec.tensor_tensor(mixed[:, :], mixed[:, :], sgb[:, :], ALU.mult).then_inc(ys_ready, 1)
                        if n == POOL_AFTER[g] + 2:
                            y_low(c, g, yp_high, yp_low, g, yP)
                        if n == SGU_AFTER[g] + 2:
                            y_low(c, g, ys_high, ys_low, G + g, mixed)
                    if n == V_UNITS + 1:
                        v_norm_of(c, 1)
                        v_stats_of(c, 2)
                        v_low_of(c, 0)
                        v_stats_of(c, 3)
                        v_norm_of(c, 2)
                        v_low_of(c, 1)
                        v_norm_of(c, 3)
                    if n == V_UNITS + 2:
                        v_low_of(c, 2)
                        v_low_of(c, 3)
                    if not last and n in X_NORM_IN:
                        x_norm_of(c + 1, X_NORM_IN[n])
                    if not last and n in X_STATS_IN:
                        x_stats_of(c + 1, X_STATS_IN[n])
                    if not last and IN_UNITS <= n < IN_UNITS + 4:
                        for k in range(2 * (n - IN_UNITS), 2 * (n - IN_UNITS) + 2):
                            h_split(c + 1, k)
                    if n >= IN_UNITS + 4:
                        j = n - IN_UNITS - 4
                        if j == 0:
                            if first:
                                dve.wait_ge(gate_ready, 2)
                                dve.wait_ge(rows_landed, 32)
                            dve.wait_ge(unit_done, c * UNITS + IN_UNITS + 4)
                        z_half(c, j, 0, A)

            run_chunks(dve, chunk)
            z_steps[1].begin(CHUNKS - 1)
            for j in range(TILES):
                dve.wait_ge(unit_done, CHUNKS * UNITS - TILES + j + 1)
                z_half(CHUNKS - 1, j, 1, B)
                if j == 1:
                    z_norm(CHUNKS - 1, 0)
                if j == 2:
                    dve.wait_ge(tail_scaled, 1)
                    vec.tensor_tensor(z[:, 1, :], z[:, 1, :], lnbB[:, :], ALU.add).then_inc(z_ready, 1)
            dve.wait_ge(tail_normed, 2)
            dve.wait_ge(tail_scaled, 2)
            vec.tensor_tensor(z[:, 2, HALF:], z[:, 2, HALF:], lngB[:, HALF:], ALU.mult).then_inc(tail_scaled, 1)
            dve.wait_ge(z_rstd, CHUNKS * TILES)
            for half in range(2):
                cut = slice(half * HALF, (half + 1) * HALF)
                zh = z[:, TILES - 1, cut]
                z_steps[1].then(dve, vec.scalar_tensor_tensor(out=zh, in0=zh, scalar=zmv[:, TILES - 1, 0:1],
                                                              in1=lngB[:, cut], op0=ALU.subtract, op1=ALU.mult))
                vec.scalar_tensor_tensor(out=zh, in0=zh, scalar=zrs[:, TILES - 1:TILES], in1=lnbB[:, cut],
                                         op0=ALU.mult, op1=ALU.add).then_inc(tail_halves, 1)

        @block.tensor
        def _(pe):
            mm = nc.tensor.matmul

            def product(bank, wh, wl, mh, ml, start, stop, passes=(0, 1, 2)):
                for n in passes:
                    last = mm(bank, wl if n == 2 else wh, ml if n == 1 else mh, start=start and n == 0,
                              stop=stop and n == 2)
                return last

            def token_unit(s, q, tiles, banks, actH, actL, j_order=range(TILES), parts=(0, 1),
                           passes=(0, 1, 2)):
                for j in j_order:
                    cut = slice(j * P, (j + 1) * P)
                    for a in parts:
                        k, row = tiles[a], slice(a * T, (a + 1) * T)
                        last = product(banks[:, j, :], actH[:, k, cut], actL[:, k, cut], wH[:, s, row], wL[:, s, row],
                                       start=(q == 0 and a == 0), stop=(q == 3 and a == 1), passes=passes)
                return last

            def channel_unit(s, bank):
                for k in range(KT):
                    cut = slice(k * P, (k + 1) * P)
                    last = product(bank, wH[:, s, cut], wL[:, s, cut], hH[:, k, :], hL[:, k, :],
                                   start=(k == 0), stop=(k == KT - 1))
                return last

            def turn(c, k, bank, j):
                return nc.tensor.transpose(B[:, bank, j * P:(j + 1) * P], xn[:, j, k * P:(k + 1) * P], ident[:, :])

            def turn_x(c, k, bank):
                for j in range(TILES):
                    last = turn(c, k, bank, j)
                last.then_inc(x_turned, 1)

            def mod_own(q, units=PE_MODS):
                wait(pe, mod_ready, q)
                if q == 0:
                    pe.wait_ge(vec_ready, 1)
                    pe.wait_ge(c_ready, 1)
                for m in units:
                    if m // 4 == q:
                        m_wait(pe, m)
                        for k in (2 * (m % 4), 2 * (m % 4) + 1):
                            for i in range(4):
                                col = (k % 2) * T + i * P
                                last = mm(B[:, 3, i:i + 1], m_slot(m)[:, col:col + P], csilu[:, k:k + 1],
                                          start=(k == 0 and i == 0), stop=False, skip_group_check=True)
                        last.then_inc(mod_multiplied, 1)

            def mod_sums(q):
                own = 4 * q in PE_MODS
                pe.wait_ge(mod_used, max(n for n, m in enumerate(DVE_MODS) if m // 4 == q) + 1)
                for i in range(4):
                    last = mm(B[:, 3, i:i + 1], macc[:, q, i * P:(i + 1) * P], ones[:, 0:1],
                              start=(i == 0 and not own), stop=True, skip_group_check=True)
                last.then_inc(mod_summed, 1)

            def mod_columns(q):
                mod_own(q)
                mod_sums(q)

            def warm(n):
                for _ in range(n):
                    mm(A[:, 0, 0:P], ident[:, :], ones[:, :], start=True, stop=True)

            def turn_w_sgu():
                pe.wait_ge(mask_ready, 1)
                pe.wait_ge(mod_ready, V_UNITS)
                for h in range(G):
                    last = nc.tensor.transpose(B[:, 3, h * P:(h + 1) * P], wsN[:, h * P:(h + 1) * P], ident[:, :])
                last.then_inc(wt_turned, 1)

            def sgu_bias():
                pe.wait_ge(small_landed, 48)
                pe.wait_ge(wt_ready, 1)
                pe.wait_ge(small_high, 1)
                for h in range(G):
                    cut = slice(h * P, (h + 1) * P)
                    mm(B[:, 3, cut], sgubB[:, cut], wtF[:, cut], start=True, stop=False)
                    last = mm(B[:, 3, cut], ones[0:1, :], bsgu_row[:, cut], start=False, stop=True)
                last.then_inc(e_done, 1)

            def pool_product(c, g):
                pe.wait_ge(p_low, c * G + g + 1)
                pe.wait_ge(v_gelu, (c + 1) * TILES)
                wait(pe, yp_ready, c * G + g - 1)
                product(A[:, g % 2, :], wpH[:, g, :], wpL[:, g, :], pH[:, :], pL[:, :],
                        start=True, stop=True).then_inc(pool_done, 1)

            def sgu_product(c, h):
                pe.wait_ge(v_low, (c + 1) * TILES)
                wait(pe, ys_mixed, c * G + h)
                cut = slice(h * P, (h + 1) * P)
                for j in range(TILES):
                    bank, at = A[:, 2 + j // 2, :], (j % 2) * 2 * P
                    mm(bank[:, at:at + 2 * P], vH[:, j, cut], wt[:, h, :, :].rearrange("p r t -> p (r t)"),
                       start=True, stop=False, skip_group_check=True)
                    last = mm(bank[:, at:at + P], vL[:, j, cut], wt[:, h, 0, :], start=False, stop=True,
                              skip_group_check=True)
                last.then_inc(sgu_done, 1)

            pe.wait_ge(vec_landed, 16)
            pe.wait_ge(const_ready, 4)
            nc.tensor.transpose(B[:, 3, 0:V_ROWS], vec_rows[:, :], ident[0:V_ROWS, 0:V_ROWS]).then_inc(vec_turned, 1)
            warm(WARM[0])
            for j in range(TILES):
                if j == TILES - 1:
                    mod_sums(0)
                pe.wait_ge(x_ready, j + 1)
                for k in range(3):
                    last = turn(0, k, k, j)
                    if j == TILES - 1:
                        last.then_inc(x_turned, 1)
                if j < 2:
                    mod_own(0, (j,))
                warm(WARM[j + 1])

            def more_h(ks):
                for k in ks:
                    pe.wait_ge(h_high, k - 2)
                    turn_x(0, k, k % 3)

            banks_of_group = ((0, xa_copied), (1, ga_gated), (2, u_gelu), (3, gb_gated))

            def chunk(c, first, last):
                for n in range(UNITS):
                    s = n % S_SLOTS
                    if not (last and n >= IN_UNITS + 4):
                        pe.wait_ge(w_low, c * UNITS + n + 1)
                    if n < V_UNITS:
                        if not (first and n == 0):
                            pe.wait_ge(h_low, c * KT + 2 * n + 2)
                        if n == 0:
                            wait(pe, z_added, c * 2 * TILES - TILES)
                        tiles = (2 * n, 2 * n + 1)
                        if first and n == 0:
                            for part in range(2):
                                if part == 1:
                                    mod_columns(1)
                                pe.wait_ge(h_high, part + 1)
                                token_unit(s, n, tiles, A, hH, hL, parts=(part,), passes=(0, 1))
                                more_h((3 + part,))
                                pe.wait_ge(h_low, part + 1)
                                done = token_unit(s, n, tiles, A, hH, hL, parts=(part,), passes=(2,))
                            done.then_inc(unit_done, 1)
                        elif first and n < V_UNITS - 1:
                            token_unit(s, n, tiles, A, hH, hL, range(MOD_TILE))
                            mod_columns(n + 1)
                            token_unit(s, n, tiles, A, hH, hL, range(MOD_TILE, TILES)).then_inc(unit_done, 1)
                        else:
                            token_unit(s, n, tiles, A, hH, hL).then_inc(unit_done, 1)
                        if first:
                            more_h(((5, 6), (7,), (), ())[n])
                    elif n < IN_UNITS:
                        g, (bank, freed) = (n - V_UNITS) // 4, banks_of_group[n % 4]
                        if g:
                            pe.wait_ge(freed, c * G + g)
                        elif first:
                            pe.wait_ge(h_high, KT)
                            if bank == 3:
                                pe.wait_ge(small_high, 3)
                        else:
                            pe.wait_ge(z_added, (c - 1) * 2 * TILES + TILES + bank + 1)
                        channel_unit(s, B[:, bank, :]).then_inc(unit_done, 1)
                        if first and n == V_UNITS:
                            turn_w_sgu()
                        if first and n == V_UNITS + 1:
                            sgu_bias()
                        if n in POOL_AFTER:
                            if first and n == POOL_AFTER[0]:
                                pe.wait_ge(small_low, 2)
                            pool_product(c, POOL_AFTER.index(n))
                        if n in SGU_AFTER:
                            sgu_product(c, SGU_AFTER.index(n))
                        if first and n == IN_UNITS - 2:
                            pe.wait_ge(gate_added, GATE_UNITS - 1)
                            pe.wait_ge(bgate_landed, 16)
                            pe.wait_ge(yp_ready, G - 1)
                            pe.wait_ge(xa_copied, G)
                            for half, bank in enumerate((A[:, 0, :], B[:, 0, :])):
                                cut = slice(half * HALF, (half + 1) * HALF)
                                mm(bank, ones[:, :], gateB[:, cut], start=True, stop=False)
                                mm(bank, ones[0:1, :], bgate_row[:, cut], start=False, stop=True)\
                                    .then_inc(gate_summed, 1)
                    else:
                        half, q = (n - IN_UNITS) // 4, (n - IN_UNITS) % 4
                        if first and n == IN_UNITS:
                            pe.wait_ge(gate_ready, 2)
                        if half == 0 and not last:
                            for k in (2 * q, 2 * q + 1):
                                if q == 0:
                                    pe.wait_ge(x_ready, (c + 2) * TILES)
                                if k < 4:
                                    pe.wait_ge(banks_of_group[k][1], (c + 1) * G)
                                else:
                                    pe.wait_ge(h_high, (c + 1) * KT + k - 3)
                                turn_x(c + 1, k, k % 4)
                        if half == 0:
                            if q == 0:
                                pe.wait_ge(yp_ready, (c + 1) * G)
                                pe.wait_ge(ys_mixed, (c + 1) * G)
                            pe.wait_ge(yp_low, c * G + q + 1)
                            pe.wait_ge(ys_low, c * G + q + 1)
                        elif q == 0:
                            if last:
                                for _, freed in banks_of_group:
                                    pe.wait_ge(freed, (c + 1) * G)
                            else:
                                pe.wait_ge(h_high, (c + 2) * KT)
                        if last and half:
                            j = q
                            for i in range(4):
                                if j == 0:
                                    pe.wait_ge(w_low, c * UNITS + IN_UNITS + 4 + i + 1)
                                done = token_unit((IN_UNITS + 4 + i) % S_SLOTS, i, (i, G + i), B, yH, yL, (j,))
                            done.then_inc(unit_done, 1)
                        else:
                            token_unit(s, q, (q, G + q), A if half == 0 else B, yH, yL).then_inc(unit_done, 1)

            run_chunks(pe, chunk)
    return nc


def kernel(x, c, w_ada, b_ada, w_in, w_pool, pool_scale, sgu_ln_g, sgu_ln_b, w_sgu, b_sgu, w_out, ln_g, ln_b):
    import numpy as np
    import concourse.bacc as bacc
    from concourse.bass_utils import run_bass_kernel_spmd

    x, c, w_ada, b_ada, w_in, w_out = (np.asarray(a) for a in (x, c, w_ada, b_ada, w_in, w_out))
    d = x.shape[-1]
    kt, half = d // P, d // 2
    wi = w_in[0].reshape(kt, P, w_in.shape[-1])
    wo = w_out[0].reshape(kt, P, d)
    col_xa, col_ga, col_u, col_v, col_gb = 0, half, 2 * half, 3 * half, 4 * half

    def by_rows(blocks):
        return np.ascontiguousarray(np.transpose(blocks, (1, 0, 2))).reshape(P, -1)

    units = [by_rows(wi[2 * q:2 * q + 2, :, col_v:col_v + T]) for q in range(V_UNITS)]
    for g in range(G):
        units += [by_rows(wi[:, :, col + g * P:col + (g + 1) * P]) for col in (col_xa, col_ga, col_u, col_gb)]
    for h in range(2):
        units += [by_rows(wo[q::G, :, h * half:(h + 1) * half]) for q in range(G)]
    wa = w_ada[0].reshape(kt, P, 3, d)
    mods = []
    for q in range(4):
        pair = wa[:, :, 0:2, 2 * q * P:2 * (q + 1) * P].reshape(kt, P, T)
        mods += [by_rows(pair[2 * r:2 * r + 2]) for r in range(4)]
    mods += [wa[k, :, 2] for k in range(kt)]
    vectors = np.concatenate([c.reshape(-1, P), b_ada[0, :2 * d].reshape(-1, P),
                              np.asarray(pool_scale)[0].reshape(-1, P), np.asarray(sgu_ln_g)[0].reshape(-1, P)])
    arrays = {
        "x": x[0],
        "w_units": np.stack(units),
        "mod_units": np.stack(mods),
        "vectors": vectors,
        "b_gate": b_ada[:, 2 * d:],
        "ln_g": np.asarray(ln_g),
        "ln_b": np.asarray(ln_b),
        "sgu_b": np.asarray(sgu_ln_b).reshape(1, -1),
        "b_sgu": np.asarray(b_sgu).reshape(1, -1),
        "w_pool": np.asarray(w_pool)[0],
        "w_sgu": np.asarray(w_sgu)[0],
    }
    arrays = {name: np.ascontiguousarray(a) for name, a in arrays.items()}
    nc = bacc.Bacc("TRN2", target_bir_lowering=False, num_devices=1)
    handles = [nc.dram_tensor("in_" + name, a.shape, mybir.dt.from_np(a.dtype), kind="ExternalInput").ap()
               for name, a in arrays.items()]
    out = nc.dram_tensor("out", x[0].shape, F32, kind="ExternalOutput").ap()
    hybrid_layer(nc, *handles, out)
    result = run_bass_kernel_spmd(nc, [{"in_" + name: a for name, a in arrays.items()}], core_ids=[0])
    return result.results[0]["out"].reshape(x.shape)
```
